# Optimizing a Trainium2 kernel written in Bass

```python
import math
import jax, jax.numpy as jnp
from jax import lax
import numpy as np

D_MODEL = 1024
BATCH = 1
SEQ = 256
DEPTH = 1

LRU_WIDTH = 1024
LRU_BLOCKS = 8
LRU_C = 8.0
CONV_WIDTH = 4
ML_HEADS = 4
ML_DQK = 64
ML_DV = 128
GD_HEADS = 8
GD_DK = 64
GD_DV = 64
CHUNK = 64
N_EXPERTS = 32
TOP_K = 4
D_FF = 1024
SWIGLU_LIMIT = 7.0
SWIGLU_ALPHA = 1.702
MOE_BLOCK = 256
N_BRANCH = 3
DN_ALPHA = (2.0 * DEPTH) ** 0.25
DN_BETA = (8.0 * DEPTH) ** -0.25
LN_EPS = 1e-5
RMS_EPS = 1e-6

ML_QK_W = ML_HEADS * ML_DQK
ML_V_W = ML_HEADS * ML_DV
GD_K_W = GD_HEADS * GD_DK
GD_V_W = GD_HEADS * GD_DV
IN_SPLITS = (LRU_WIDTH, LRU_WIDTH, ML_QK_W, ML_QK_W, ML_V_W, ML_HEADS, ML_HEADS, ML_V_W,
             GD_K_W, GD_K_W, GD_V_W, GD_HEADS, GD_HEADS, GD_V_W, N_BRANCH * D_MODEL)
D_IN = sum(IN_SPLITS)
SPLIT_POINTS = [int(c) for c in np.cumsum(IN_SPLITS)[:-1]]

kernel_name = 'hybrid_lru_mlstm_gdn_moe_deepnorm'

def layer_norm(x, g, b):
    xf = x.astype(jnp.float32)
    mu = jnp.mean(xf, -1, keepdims=True)
    xc = xf - mu
    var = jnp.mean(xc * xc, -1, keepdims=True)
    return (xc * lax.rsqrt(var + LN_EPS) * g + b).astype(x.dtype)

def rms_norm(x, g):
    xf = x.astype(jnp.float32)
    return xf * lax.rsqrt(jnp.mean(xf * xf, -1, keepdims=True) + RMS_EPS) * g

def l2_norm(x):
    xf = x.astype(jnp.float32)
    return xf * lax.rsqrt(jnp.sum(xf * xf, -1, keepdims=True) + RMS_EPS)

def causal_conv(x, w):
    S = x.shape[1]
    W = w.shape[0]
    xp = jnp.pad(x, ((0, 0), (W - 1, 0), (0, 0)))
    y = xp[:, W - 1:W - 1 + S] * w[W - 1]
    for j in range(W - 1):
        y = y + xp[:, j:j + S] * w[j]
    return y

def to_chunks(t):
    B, S, H = t.shape[:3]
    t = t.reshape((B, S // CHUNK, CHUNK, H) + t.shape[3:])
    return jnp.moveaxis(t, 3, 1)

def from_chunks(t):
    B, H, NC, L, d = t.shape
    return jnp.moveaxis(t, 1, 3).reshape(B, NC * L, H, d)

def rg_lru(x, wa, ba, wx, bx, lam):
    B, S, W = x.shape
    xf = x.astype(jnp.float32)
    xb = xf.reshape(B, S, LRU_BLOCKS, W // LRU_BLOCKS)
    r = jax.nn.sigmoid(jnp.einsum('bshi,hij->bshj', xb, wa.astype(jnp.float32)) + ba).reshape(B, S, W)
    ig = jax.nn.sigmoid(jnp.einsum('bshi,hij->bshj', xb, wx.astype(jnp.float32)) + bx).reshape(B, S, W)
    log_a = -LRU_C * r * jax.nn.softplus(-lam.astype(jnp.float32))
    a = jnp.exp(log_a)
    u = jnp.sqrt(-jnp.expm1(2.0 * log_a)) * (ig * xf)
    _, h = lax.associative_scan(lambda e1, e2: (e1[0] * e2[0], e2[0] * e1[1] + e2[1]), (a, u), axis=1)
    return h

def mlstm_chunkwise(q, k, v, i_pre, f_pre):
    f32 = jnp.float32
    q = to_chunks(q.astype(f32)) * (q.shape[-1] ** -0.5)
    k = to_chunks(k.astype(f32))
    v = to_chunks(v.astype(f32))
    ig = to_chunks(i_pre.astype(f32))
    logf = to_chunks(jax.nn.log_sigmoid(f_pre.astype(f32)))
    Bn, H, NC, L, dqk = q.shape
    dv = v.shape[-1]
    b = jnp.cumsum(logf, axis=-1)
    b_last = b[..., -1]
    g_end = b_last[..., None] - b + ig

    def step(carry, inp):
        C, n, m = carry
        bl, ge, kc, vc = inp
        m_new = jnp.maximum(bl + m, jnp.max(ge, axis=-1))
        decay = jnp.exp(bl + m - m_new)
        w = jnp.exp(ge - m_new[..., None])
        C_new = decay[..., None, None] * C + jnp.einsum('bhl,bhld,bhle->bhde', w, kc, vc)
        n_new = decay[..., None] * n + jnp.einsum('bhl,bhld->bhd', w, kc)
        return (C_new, n_new, m_new), (C, n, m)

    init = (jnp.zeros((Bn, H, dqk, dv), f32), jnp.zeros((Bn, H, dqk), f32), jnp.zeros((Bn, H), f32))
    xs = tuple(jnp.moveaxis(t, 2, 0) for t in (b_last, g_end, k, v))
    _, (C_prev, n_prev, m_prev) = lax.scan(step, init, xs)
    C_prev = jnp.moveaxis(C_prev, 0, 2)
    n_prev = jnp.moveaxis(n_prev, 0, 2)
    m_prev = jnp.moveaxis(m_prev, 0, 2)

    causal = jnp.tril(jnp.ones((L, L), bool))
    D = jnp.where(causal, b[..., :, None] - b[..., None, :] + ig[..., None, :], -jnp.inf)
    inter = b + m_prev[..., None]
    m_t = jnp.maximum(inter, jnp.max(D, axis=-1))
    Dw = jnp.exp(D - m_t[..., None])
    iw = jnp.exp(inter - m_t)
    s = jnp.einsum('bhcld,bhcsd->bhcls', q, k) * Dw
    num = jnp.einsum('bhcls,bhcse->bhcle', s, v) + iw[..., None] * jnp.einsum('bhcld,bhcde->bhcle', q, C_prev)
    den = jnp.sum(s, axis=-1) + iw * jnp.einsum('bhcld,bhcd->bhcl', q, n_prev)
    h = num / jnp.maximum(jnp.abs(den), jnp.exp(-m_t))[..., None]
    return from_chunks(h)

def gated_delta_chunked(q, k, v, g, beta):
    f32 = jnp.float32
    q = to_chunks(q.astype(f32)) * (q.shape[-1] ** -0.5)
    k = to_chunks(k.astype(f32))
    v = to_chunks(v.astype(f32))
    g = to_chunks(g.astype(f32))
    beta = to_chunks(beta.astype(f32))
    Bn, H, NC, L, dk = q.shape
    dv = v.shape[-1]
    gc = jnp.cumsum(g, axis=-1)
    causal = jnp.tril(jnp.ones((L, L), bool))
    strict = jnp.tril(jnp.ones((L, L), bool), k=-1)
    gam = jnp.exp(jnp.where(causal, gc[..., :, None] - gc[..., None, :], -jnp.inf))
    a_mat = jnp.where(strict, beta[..., :, None] * gam * jnp.einsum('bhcld,bhcsd->bhcls', k, k), 0.0)
    eye = jnp.eye(L, dtype=f32)
    rhs = jnp.concatenate([beta[..., None] * v, (beta * jnp.exp(gc))[..., None] * k], axis=-1)
    sol = lax.linalg.triangular_solve(eye + a_mat, rhs, left_side=True, lower=True, unit_diagonal=True)
    u, w = sol[..., :dv], sol[..., dv:]
    p = gam * jnp.einsum('bhcld,bhcsd->bhcls', q, k)
    qg = q * jnp.exp(gc)[..., None]
    kd = k * jnp.exp(gc[..., -1:] - gc)[..., None]
    gl = jnp.exp(gc[..., -1])

    def step(S, inp):
        qg_c, p_c, u_c, w_c, kd_c, gl_c = inp
        delta = u_c - jnp.einsum('bhld,bhde->bhle', w_c, S)
        o = jnp.einsum('bhld,bhde->bhle', qg_c, S) + jnp.einsum('bhls,bhse->bhle', p_c, delta)
        S_new = gl_c[..., None, None] * S + jnp.einsum('bhld,bhle->bhde', kd_c, delta)
        return S_new, o

    xs = tuple(jnp.moveaxis(t, 2, 0) for t in (qg, p, u, w, kd, gl))
    _, o = lax.scan(step, jnp.zeros((Bn, H, dk, dv), f32), xs)
    return from_chunks(jnp.moveaxis(o, 0, 2))

def token_mixers(x, w_in, lru_conv_w, lru_conv_b, lru_wa, lru_ba, lru_wx, lru_bx, lru_lambda,
                 ml_i_bias, ml_f_bias, ml_norm_g, gd_conv_w, gd_a_log, gd_dt_bias, gd_norm_g,
                 w_br_lru, w_br_ml, w_br_gd, w_out):
    B, S, _ = x.shape
    f32 = jnp.float32
    proj = x @ w_in
    (lru_x, lru_y, ml_q, ml_k, ml_v, ml_i, ml_f, ml_o,
     gd_q, gd_k, gd_v, gd_a, gd_b, gd_z, gate_pre) = jnp.split(proj, SPLIT_POINTS, axis=-1)

    xa = causal_conv(lru_x, lru_conv_w) + lru_conv_b
    ha = rg_lru(xa, lru_wa, lru_ba, lru_wx, lru_bx, lru_lambda) * jax.nn.gelu(lru_y.astype(f32))
    br_a = ha.astype(x.dtype) @ w_br_lru

    hb = mlstm_chunkwise(ml_q.reshape(B, S, ML_HEADS, ML_DQK), ml_k.reshape(B, S, ML_HEADS, ML_DQK),
                         ml_v.reshape(B, S, ML_HEADS, ML_DV), ml_i + ml_i_bias, ml_f + ml_f_bias)
    hb = rms_norm(hb, ml_norm_g) * jax.nn.sigmoid(ml_o.astype(f32)).reshape(B, S, ML_HEADS, ML_DV)
    br_b = hb.reshape(B, S, ML_V_W).astype(x.dtype) @ w_br_ml

    qkv = jax.nn.silu(causal_conv(jnp.concatenate([gd_q, gd_k, gd_v], axis=-1), gd_conv_w))
    q, k, v = jnp.split(qkv, [GD_K_W, 2 * GD_K_W], axis=-1)
    q = l2_norm(q.reshape(B, S, GD_HEADS, GD_DK))
    k = l2_norm(k.reshape(B, S, GD_HEADS, GD_DK))
    g = -jnp.exp(gd_a_log) * jax.nn.softplus(gd_a.astype(f32) + gd_dt_bias)
    beta = jax.nn.sigmoid(gd_b.astype(f32))
    hc = gated_delta_chunked(q, k, v.reshape(B, S, GD_HEADS, GD_DV), g, beta)
    hc = rms_norm(hc, gd_norm_g) * jax.nn.silu(gd_z.astype(f32)).reshape(B, S, GD_HEADS, GD_DV)
    br_c = hc.reshape(B, S, GD_V_W).astype(x.dtype) @ w_br_gd

    gates = jax.nn.sigmoid(gate_pre.astype(f32)).reshape(B, S, N_BRANCH, D_MODEL)
    merged = gates[..., 0, :] * br_a + gates[..., 1, :] * br_b + gates[..., 2, :] * br_c
    return (merged.astype(x.dtype) @ w_out).astype(x.dtype)

def moe_ffn(x, router_w, router_b, w1, b1, w2, b2):
    B, S, D = x.shape
    T = B * S
    A = T * TOP_K
    xf = x.reshape(T, D)
    logits = (xf @ router_w + router_b).astype(jnp.float32)
    top_val, top_idx = lax.top_k(logits, TOP_K)
    gate = jax.nn.softmax(top_val, axis=-1)
    flat_e = top_idx.reshape(A)
    flat_tok = jnp.repeat(jnp.arange(T, dtype=jnp.int32), TOP_K)
    flat_w = gate.reshape(A)
    order = jnp.argsort(flat_e)
    sorted_e = flat_e[order]
    counts = jnp.bincount(flat_e, length=N_EXPERTS)
    padded = ((counts + MOE_BLOCK - 1) // MOE_BLOCK) * MOE_BLOCK
    pad_end = jnp.cumsum(padded)
    pad_start = pad_end - padded
    start = jnp.cumsum(counts) - counts
    dest = pad_start[sorted_e] + (jnp.arange(A, dtype=jnp.int32) - start[sorted_e])
    n_blocks = -(-A // MOE_BLOCK) + N_EXPERTS
    P = n_blocks * MOE_BLOCK
    tok_buf = jnp.full((P,), T, jnp.int32).at[dest].set(flat_tok[order])
    w_buf = jnp.zeros((P,), jnp.float32).at[dest].set(flat_w[order])
    block_e = jnp.clip(jnp.searchsorted(pad_end, jnp.arange(n_blocks) * MOE_BLOCK, side='right'), 0, N_EXPERTS - 1)
    x_pad = jnp.concatenate([xf, jnp.zeros((1, D), xf.dtype)], axis=0)

    def expert_block(args):
        tok, e = args
        hdn = x_pad[tok] @ w1[e] + b1[e]
        glu, lin = hdn[:, :D_FF], hdn[:, D_FF:]
        glu = jnp.minimum(glu, SWIGLU_LIMIT)
        lin = jnp.clip(lin, -SWIGLU_LIMIT, SWIGLU_LIMIT)
        act = glu * jax.nn.sigmoid(SWIGLU_ALPHA * glu) * (lin + 1.0)
        return act @ w2[e] + b2[e]

    y = lax.map(expert_block, (tok_buf.reshape(n_blocks, MOE_BLOCK), block_e)).reshape(P, D)
    y = y * w_buf[:, None].astype(y.dtype)
    out = jnp.zeros((T + 1, D), y.dtype).at[tok_buf].add(y)[:T]
    return out.reshape(B, S, D).astype(x.dtype)

def setup_inputs(seed: int = 0) -> dict:
    key = jax.random.key(seed)
    ks = iter(jax.random.split(key, 40))
    f32 = jnp.float32

    def nrm(shape, scale):
        return scale * jax.random.normal(next(ks), shape, f32)

    def unif(shape, lo, hi):
        return jax.random.uniform(next(ks), shape, f32, lo, hi)

    Lr = DEPTH
    bw = LRU_WIDTH // LRU_BLOCKS
    gd_ch = 2 * GD_K_W + GD_V_W
    a_base = unif((Lr, LRU_WIDTH), 0.9, 0.999) ** (1.0 / LRU_C)
    dt = jnp.exp(unif((Lr, GD_HEADS), math.log(1e-3), math.log(0.1)))
    return {
        'x': nrm((BATCH, SEQ, D_MODEL), 1.0),
        'w_in': nrm((Lr, D_MODEL, D_IN), D_MODEL ** -0.5),
        'lru_conv_w': nrm((Lr, CONV_WIDTH, LRU_WIDTH), CONV_WIDTH ** -0.5),
        'lru_conv_b': nrm((Lr, LRU_WIDTH), 0.02),
        'lru_wa': nrm((Lr, LRU_BLOCKS, bw, bw), bw ** -0.5),
        'lru_ba': nrm((Lr, LRU_BLOCKS, bw), 0.02),
        'lru_wx': nrm((Lr, LRU_BLOCKS, bw, bw), bw ** -0.5),
        'lru_bx': nrm((Lr, LRU_BLOCKS, bw), 0.02),
        'lru_lambda': jnp.log(a_base) - jnp.log1p(-a_base),
        'ml_i_bias': -2.0 + nrm((Lr, ML_HEADS), 0.1),
        'ml_f_bias': jnp.linspace(3.0, 6.0, ML_HEADS)[None, :] + nrm((Lr, ML_HEADS), 0.1),
        'ml_norm_g': 1.0 + nrm((Lr, ML_HEADS, ML_DV), 0.02),
        'gd_conv_w': nrm((Lr, CONV_WIDTH, gd_ch), CONV_WIDTH ** -0.5),
        'gd_a_log': jnp.log(unif((Lr, GD_HEADS), 1.0, 16.0)),
        'gd_dt_bias': dt + jnp.log(-jnp.expm1(-dt)),
        'gd_norm_g': 1.0 + nrm((Lr, GD_DV), 0.02),
        'w_br_lru': nrm((Lr, LRU_WIDTH, D_MODEL), DN_BETA * LRU_WIDTH ** -0.5),
        'w_br_ml': nrm((Lr, ML_V_W, D_MODEL), DN_BETA * ML_V_W ** -0.5),
        'w_br_gd': nrm((Lr, GD_V_W, D_MODEL), DN_BETA * GD_V_W ** -0.5),
        'w_out': nrm((Lr, D_MODEL, D_MODEL), DN_BETA * D_MODEL ** -0.5),
        'ln1_g': 1.0 + nrm((Lr, D_MODEL), 0.02),
        'ln1_b': nrm((Lr, D_MODEL), 0.02),
        'router_w': nrm((Lr, D_MODEL, N_EXPERTS), D_MODEL ** -0.5),
        'router_b': nrm((Lr, N_EXPERTS), 0.01),
        'exp_w1': nrm((Lr, N_EXPERTS, D_MODEL, 2 * D_FF), D_MODEL ** -0.5),
        'exp_b1': nrm((Lr, N_EXPERTS, 2 * D_FF), 0.02),
        'exp_w2': nrm((Lr, N_EXPERTS, D_FF, D_MODEL), DN_BETA * D_FF ** -0.5),
        'exp_b2': nrm((Lr, N_EXPERTS, D_MODEL), 0.02),
        'ln2_g': 1.0 + nrm((Lr, D_MODEL), 0.02),
        'ln2_b': nrm((Lr, D_MODEL), 0.02),
    }

def reference(x, w_in, lru_conv_w, lru_conv_b, lru_wa, lru_ba, lru_wx, lru_bx, lru_lambda,
              ml_i_bias, ml_f_bias, ml_norm_g, gd_conv_w, gd_a_log, gd_dt_bias, gd_norm_g,
              w_br_lru, w_br_ml, w_br_gd, w_out, ln1_g, ln1_b, router_w, router_b,
              exp_w1, exp_b1, exp_w2, exp_b2, ln2_g, ln2_b):
    for l in range(DEPTH):
        y = token_mixers(x, w_in[l], lru_conv_w[l], lru_conv_b[l], lru_wa[l], lru_ba[l], lru_wx[l],
                         lru_bx[l], lru_lambda[l], ml_i_bias[l], ml_f_bias[l], ml_norm_g[l],
                         gd_conv_w[l], gd_a_log[l], gd_dt_bias[l], gd_norm_g[l],
                         w_br_lru[l], w_br_ml[l], w_br_gd[l], w_out[l])
        x = layer_norm(DN_ALPHA * x + y, ln1_g[l], ln1_b[l])
        y = moe_ffn(x, router_w[l], router_b[l], exp_w1[l], exp_b1[l], exp_w2[l], exp_b2[l])
        x = layer_norm(DN_ALPHA * x + y, ln2_g[l], ln2_b[l])
    return x


_drawn_inputs = setup_inputs


def setup_inputs(seed=0):
    import zlib

    import numpy as np

    out = dict(_drawn_inputs(seed))
    spreads = {}
    factors = {'lru_conv_b': 3.362,
     'lru_ba': 124.359,
     'lru_bx': 32.302,
     'ml_i_bias': 64.0,
     'ml_norm_g': 44.992,
     'gd_norm_g': 8.0,
     'router_b': 5.165,
     'exp_b1': 8.0,
     'exp_b2': 6.406,
     'ln2_g': 20.519,
     'ln2_b': 21.974,
     'lru_wa': 2.73,
     'ml_f_bias': 8.0,
     'w_br_ml': 8.0}
    for name, (base, spread) in spreads.items():
        noise = np.random.default_rng([zlib.crc32(name.encode()), seed]).standard_normal(out[name].shape)
        drawn = base * np.exp(spread * noise) if base else spread * noise
        out[name] = __import__('jax').numpy.asarray(drawn.astype(out[name].dtype))
    for name, factor in factors.items():
        out[name] = (out[name] * factor).astype(out[name].dtype)
    return out
```

```python
from contextlib import ExitStack

import numpy as np

import concourse.bass as bass
from concourse import mybir

F32 = mybir.dt.float32
I32 = mybir.dt.int32
ALU = mybir.AluOpType
ACT = mybir.ActivationFunctionType
AX = mybir.AxisListType

P = 128
S = 256
NT = S // P
D = 1024
KD = D // P
LW = 1024
NB = LW // P
MH, MQ, MV = 4, 64, 128
GH, GK = 8, 64
GP = GH // 2
CH = 64
NC = S // CH
NE, TOPK, FF = 32, 4, 1024
KF = FF // P
CAP = 64
ROUNDS = S // CAP
LRU_C = 8.0
ALPHA = 2.0 ** 0.25
LN_EPS, RMS_EPS = 1e-5, 1e-6
LIMIT, SWIGLU = 7.0, 1.702
NEG = -1e30

C_LX, C_LY = 0, LW
C_MQ = 2 * LW
C_MK = C_MQ + MH * MQ
C_MV = C_MK + MH * MQ
C_MI = C_MV + MH * MV
C_MO = C_MI + 2 * MH
C_GQ = C_MO + MH * MV
C_GK = C_GQ + GH * GK
C_GV = C_GK + GH * GK
C_GA = C_GV + GH * GK
C_GZ = C_GA + 2 * GH
C_GT = C_GZ + GH * GK
D_IN = C_GT + 3 * D

GW = 256
WBUFS = 3

(K_ID, K_BLK, K_L0T, K_L1, K_L2, K_L3, K_L4, K_L5, K_MTRI, K_GTRI, K_BEFORE, K_ONES, K_IOTA,
 K_COLS, K_RST0, K_RST1) = range(16)
NPLANES = 16

V_CW, V_CB, V_BA, V_BX, V_LAM, V_GCW, V_MG, V_GG = 0, 32, 40, 48, 56, 64, 112, 116
NVEC = 117


def constant_planes():
    c = np.zeros((P, NPLANES, P), np.float32)
    r, q = np.arange(P)[:, None], np.arange(P)[None, :]
    c[:, K_ID] = r == q
    c[:, K_BLK] = r // CH == q // CH
    c[:, K_L0T] = (q % 2 == 1) & (r == q - 1)
    for k in range(1, 6):
        b = 2 ** k
        c[:, K_L0T + k] = ((r // b) % 2 == 1) & (q // b == r // b - 1)
    c[:, K_MTRI] = np.where(r <= q, 0.0, NEG)
    c[:, K_GTRI] = np.where((r <= q) & (r // CH == q // CH), 0.0, NEG)
    c[:, K_BEFORE] = r < q
    c[:, K_ONES] = 1.0
    c[:, K_IOTA] = q % CAP + 0 * r
    c[:, K_COLS, 0:1] = np.where((r >= 32) & (r < 64), -1.0, 1.0)
    c[:, K_COLS, 1:2] = np.where((r >= 32) & (r < 96), -1.0, 0.0)
    reset = np.ones((P, S), np.float32)
    reset[64:96, ::CH] = 0.0
    c[:, K_RST0:K_RST1 + 1] = reset.reshape(P, 2, P)
    return c.reshape(P, NPLANES * P)


def weight_stream():
    seq = [(f"gq{n}", "w_in", C_GQ + GW * n) for n in range(6)]
    seq += [(f"lx{n}", "w_in", C_LX + GW * n) for n in range(4)]
    seq += [(f"ly{n}", "w_in", C_LY + GW * n) for n in range(4)]
    seq += [("mq", "w_in", C_MQ), ("mk", "w_in", C_MK)]
    seq += [(f"mv{n}", "w_in", C_MV + GW * n) for n in range(2)]
    seq += [(f"mo{n}", "w_in", C_MO + GW * n) for n in range(2)]
    seq += [(f"gz{n}", "w_in", C_GZ + GW * n) for n in range(2)]
    for n in range(3):
        for d in range(4):
            seq += [(f"ga{n}{d}", "w_in", C_GT + D * n + GW * d),
                    (f"br{n}{d}", ("w_br_lru", "w_br_ml", "w_br_gd")[n], GW * d)]
    seq += [(f"wo{d}", "w_out", GW * d) for d in range(4)]
    return seq


def bank_uses():
    order = [(f"xT{n}", n) for n in range(4)] + [("vec", 4), ("small", 5)]
    proj = 0

    def p(name):
        nonlocal proj
        order.append((name, proj % 4))
        proj += 1
    for n in range(6):
        p(f"gq{n}")
    for n in range(4):
        p(f"lx{n}")
    order.append(("rc", 6))
    order += [("ss0", 4), ("ss1", 5), ("ss2", 6), ("ss3", 7)]
    order += [("bb0", 4), ("bb1", 5), ("gb0", 6), ("gb1", 7)]
    order += [("vt0", 4), ("vt1", 5), ("kt0", 6), ("kt1", 7)]
    order += [(f"gr{n}", 4 + n) for n in range(4)]
    order += [(f"at{n}", 4 + n) for n in range(4)]
    order += [(f"pt{n}", 4 + n) for n in range(4)]
    order += [(f"x1{n}", 4 + n) for n in range(4)]
    filler = [f"ly{n}" for n in range(4)] + ["mq", "mk", "mv0", "mv1", "mo0", "mo1", "gz0", "gz1"]
    for k in range(1, 6):
        order += [(f"y{k}{n}", 4 + n) for n in range(4)]
        p(filler[2 * k - 2])
        if k < 5:
            order += [(f"z{k}{n}", 4 + n) for n in range(4)]
        order += [(f"t{k}{n}", 4 + n) for n in range(4)]
        p(filler[2 * k - 1])
    order += [("u0", 4), ("u1", 5), ("w0", 6), ("w1", 7)]
    p("gz0")
    p("gz1")
    lru = [(f"lg{b}", b % 4) for b in range(NB)]
    for c in range(NC):
        order += [(f"ws{c}", 4)]
        order += lru[2 * c:2 * c + 2]
        if c % 2 == 0:
            order += [(f"o{c // 2}", 5 + c // 2)]
        order += [(f"sn{c}", 7)]
    order += [("ot0", 4), ("ot1", 7)]
    order += [("mr0", 5), ("mr1", 6)]
    order += [("ms00", 4), ("ms10", 7), ("ms01", 5), ("ms11", 6)]
    order += [("mn00", 4), ("mn01", 7), ("mn10", 5), ("mn11", 6)]
    order += [("mt0", 4), ("mt1", 7)]
    k = 0
    for n in (0, 1, 2):
        for d in range(4):
            order += [(f"ga{n}{d}", k % 4), (f"br{n}{d}", (k + 1) % 4)]
            k += 2
    order += [(f"wo{d}", d) for d in range(4)]
    order += [(f"x1T{n}", 4 + n) for n in range(4)]
    order += [("lgt", 0), ("cnt", 1), ("gT", 3)]
    count = [0] * 8
    uses = {}
    for name, bank in order:
        count[bank] += 1
        assert name not in uses, name
        uses[name] = (bank, count[bank])
    return uses, count


def layer_kernel(nc, stop, dump, x, w_in, lru_conv_w, lru_conv_b, lru_wa, lru_ba, lru_wx, lru_bx,
                 lru_lambda, ml_i_bias, ml_f_bias, ml_norm_g, gd_conv_w, gd_a_log, gd_dt_bias,
                 gd_norm_g, w_br_lru, w_br_ml, w_br_gd, w_out, ln1_g, ln1_b, router_w, router_b,
                 exp_w1, exp_b1, exp_w2, exp_b2, ln2_g, ln2_b, planes, out):
    uses, bank_total = bank_uses()
    stream = weight_stream()
    stream_at = {name: n for n, (name, _, _) in enumerate(stream)}
    sources = {"w_in": w_in, "w_br_lru": w_br_lru, "w_br_ml": w_br_ml, "w_br_gd": w_br_gd,
               "w_out": w_out}
    with ExitStack() as ctx:
        sems = {}

        def E(name):
            if name not in sems:
                sems[name] = ctx.enter_context(nc.semaphore("s_" + name))
            return sems[name]

        RING = ctx.enter_context(nc.sbuf_tensor("ring", [P, 96 * 256], F32))
        MIX = ctx.enter_context(nc.sbuf_tensor("mix", [P, 28400], F32))
        NR = ctx.enter_context(nc.sbuf_tensor("rounds", [P, 1], I32))
        PS = ctx.enter_context(nc.psum_tensor("ps", [P, 8, 512], F32))

        def area(base, kb, words):
            return base[:, int(kb * 256):int(kb * 256) + words]

        WB = [area(MIX, 8 * n, 2048).rearrange("p (c n) -> p c n", n=GW) for n in range(WBUFS)]
        XTOK = area(MIX, 24, 2048).rearrange("p (t d) -> p t d", t=NT)
        XT = area(MIX, 32, 2048).rearrange("p (c s) -> p c s", s=S)
        LX = area(MIX, 40, NB * 259).rearrange("p (b s) -> p b s", s=259)
        LY = area(MIX, 48.25, 2048).rearrange("p (b s) -> p b s", s=S)
        XA = area(MIX, 56.25, 2048).rearrange("p (b s) -> p b s", s=S)
        GZ = area(MIX, 64.25, 1024).rearrange("p (j s) -> p j s", s=S)
        MO = area(MIX, 68.25, 1024).rearrange("p (j s) -> p j s", s=S)
        V1 = area(MIX, 72.25, NT * MH * 129).rearrange("p (t h e) -> p t h e", t=NT, h=MH)
        QM = area(MIX, 76.5, 1024).rearrange("p (j a s) -> p j a s", j=2, a=2)
        MK = area(MIX, 80.5, 512).rearrange("p (j s) -> p j s", s=S)
        HB = area(MIX, 82.5, 1024).rearrange("p (j s) -> p j s", s=S)
        HC = area(MIX, 86.5, 1024).rearrange("p (j s) -> p j s", s=S)
        CM = area(MIX, 90.5, NPLANES * P).rearrange("p (k n) -> p k n", n=P)
        VR = area(MIX, 98.5, P)
        VC = area(MIX, 99, P)
        RB = area(MIX, 99.5, S)
        RW = area(MIX, 100.5, S)
        RX = area(MIX, 101.5, S)
        NM = area(MIX, 102.5, S)
        ROUT = area(MIX, 103.5, 256).rearrange("p (c e) -> p c e", e=NE)
        RC = area(MIX, 104.5, 512).rearrange("p (t k n) -> p t k n", t=2, k=2)
        B2 = area(MIX, 106.5, 1024)
        SC = area(MIX, 110.5, 110)
        RBIAS = SC[:, 0:32]
        BIAS, ALOG, COEF = SC[:, 32:33], SC[:, 33:34], SC[:, 34:35]
        LSP = SC[:, 40:48]
        NLSP = SC[:, 48:56]
        BG = SC[:, 56:72].rearrange("p (t h) -> p t h", t=NT)
        TS = SC[:, 72:104]
        ident = CM[:, K_ID]

        GIN = area(RING, 0, 12 * 259).rearrange("p (b s) -> p b s", s=259)
        X_ = area(RING, 0, 2048).rearrange("p (n q) -> p n q", q=512)
        XTi = area(RING, 8, 2048).rearrange("p (n q) -> p n q", q=512)
        AT = area(RING, 16, 2048).rearrange("p (n q) -> p n q", q=512)
        Y_ = area(RING, 24, 2048).rearrange("p (n q) -> p n q", q=512)
        GCO = area(RING, 16, 12 * S).rearrange("p (b s) -> p b s", s=S)
        GSIG = area(RING, 48, 12 * S).rearrange("p (b s) -> p b s", s=S)
        GAM = area(RING, 32, 2048).rearrange("p (n q) -> p n q", q=512)
        PT = area(RING, 40, 2048).rearrange("p (n q) -> p n q", q=512)
        ROWT = [area(RING, 32 + n, S) for n in range(8)]
        QB = area(RING, 48, 2048).rearrange("p (j a s) -> p j a s", j=GP, a=2)
        KB = area(RING, 56, 2048).rearrange("p (j a s) -> p j a s", j=GP, a=2)
        QG = area(RING, 64, 1024).rearrange("p (j s) -> p j s", s=S)
        KT = area(RING, 68, 1024).rearrange("p (j s) -> p j s", s=S)
        KBE = area(RING, 72, 1024).rearrange("p (t n) -> p t n", t=NT)
        KDE = area(RING, 76, 1024).rearrange("p (t n) -> p t n", t=NT)
        BV = area(RING, 80, 1024).rearrange("p (t n) -> p t n", t=NT)
        EG = area(RING, 84, 1024).rearrange("p (j s) -> p j s", s=S)
        RN = area(RING, 88, 2048).rearrange("p (b s) -> p b s", s=S)
        WSM = area(RING, 88, 1024).rearrange("p (c n) -> p c n", n=P)
        SQ = area(RING, 40, 2048).rearrange("p (b s) -> p b s", s=S)
        U_ = area(RING, 48, 1024).rearrange("p (t n) -> p t n", t=NT)
        WT = area(RING, 52, 1024).rearrange("p (t j n) -> p t j n", t=NT, j=GP)
        DE = area(RING, 56, 1024).rearrange("p (t n) -> p t n", t=NT)
        ST = area(RING, 60, 512)
        STT = area(RING, 62, 512)
        OS = area(RING, 24, 1024).rearrange("p (t n) -> p t n", t=NT)
        OQ = area(RING, 28, 1024).rearrange("p (t n) -> p t n", t=NT)
        LR = area(RING, 0, 2048).rearrange("p (b s) -> p b s", s=S)
        LG = area(RING, 8, 2048).rearrange("p (b s) -> p b s", s=S)
        LA = area(RING, 16, 2048).rearrange("p (b s) -> p b s", s=S)
        LU = area(RING, 32, 2048).rearrange("p (b s) -> p b s", s=S)
        LT = area(MIX, 40, 2048).rearrange("p (b s) -> p b s", s=S)
        LWA = area(RING, 88, 1024).rearrange("p (b n) -> p b n", n=P)
        LWX = area(RING, 92, 1024).rearrange("p (b n) -> p b n", n=P)
        ME = area(RING, 48, 1536).rearrange("p (h b n) -> p h b n", h=MH, b=3)
        MS = area(RING, 54, 1536).rearrange("p (h b n) -> p h b n", h=MH, b=3)
        MN = area(RING, 60, 1024).rearrange("p (t h n) -> p t h n", t=NT, h=MH)
        MQ2 = area(RING, 64, 1024).rearrange("p (t h n) -> p t h n", t=NT, h=MH)
        MG = area(MIX, 56.25, 2048).rearrange("p (c s) -> p c s", s=S)
        SG = [area(RING, 72 + 2 * n, 512) for n in range(2)]
        MT = [area(RING, 76 + 2 * n, 512) for n in range(2)]
        X1 = area(MIX, 40, 2048).rearrange("p (t d) -> p t d", t=NT)
        LNG = area(MIX, 64.25, 1024)
        LNB = area(MIX, 68.25, 1024)
        X1T = area(MIX, 32, 2048).rearrange("p (c s) -> p c s", s=S)
        B1R = area(MIX, 72.25, 2048)
        W1 = RING[:, 0:KD * 2 * FF].rearrange("p (c n) -> p c n", n=2 * FF)
        W2 = RING[:, KD * 2 * FF:].rearrange("p (c n) -> p c n", n=D)
        XG = area(MIX, 0, 512)
        XE = area(MIX, 2, 512).rearrange("p (q n) -> p q n", q=4)
        GLU = area(MIX, 4, 512)
        LIN = area(MIX, 6, 512)
        SIG = area(MIX, 8, 512)
        HID = area(MIX, 10, 512)
        HT = area(MIX, 12, 512).rearrange("p (q n) -> p q n", q=4)
        YS = area(MIX, 14, 512)
        ONE = area(MIX, 16, NT * CAP).rearrange("p (t n) -> p t n", t=NT)
        GAD = area(MIX, 16.5, NT * P).rearrange("p (t n) -> p t n", t=NT)
        GTS = area(MIX, 17.5, S)
        PICK = area(MIX, 18.5, CAP)
        POS = area(MIX, 20, NT * 129).rearrange("p (t n) -> p t n", t=NT)
        GAT = area(MIX, 21.25, NT * 129).rearrange("p (t n) -> p t n", t=NT)
        LOG = area(MIX, 82.5, 80).rearrange("p (t e) -> p t e", t=NT)
        LOGR = area(MIX, 86, 80).rearrange("p (t e) -> p t e", t=NT)
        SEL = area(MIX, 83, 64).rearrange("p (t e) -> p t e", t=NT)
        EXL = area(MIX, 83.25, 64).rearrange("p (t e) -> p t e", t=NT)
        TOP = area(MIX, 83.5, 16).rearrange("p (t e) -> p t e", t=NT)
        GTT = area(MIX, 84, 256)
        RT2 = area(MIX, 85, 64)

        locals_ = dict(locals())

        def ps(name):
            return PS[:, uses[name][0], :]

        nc_v, nc_s, nc_g = nc.vector, nc.scalar, nc.gpsimd
        block = ctx.enter_context(nc.Block())

        def full(eng, name):
            bank, n = uses[name]
            eng.wait_ge(E(f"bank_full{bank}"), n)

        def moved(eng, name):
            bank, n = uses[name]
            eng.wait_ge(E(f"bank_free{bank}"), n)

        def free(name):
            return E(f"bank_free{uses[name][0]}")

        @block.sync
        def _(sp):
            sp.dma_start(XTOK, x[0].rearrange("(t p) d -> p t d", p=P)).then_inc(E("x_in"), 16)
            for n, (name, src, col) in enumerate(stream):
                w = sources[src][0]
                k = w.shape[0] // P
                if n >= WBUFS:
                    full(sp, stream[n - WBUFS][0])
                sp.dma_start(WB[n % WBUFS][:, 0:k, :],
                             w[:, col:col + GW].rearrange("(c p) n -> p c n", p=P)
                             ).then_inc(E(f"w_in{n % WBUFS}"), 16)
                if name == "gz1":
                    sp.wait_ge(E("rn_done"), 1)
                    sp.dma_start(LWA, lru_wa[0].rearrange("b i j -> i b j")).then_inc(E("lwa"), 16)
                    sp.dma_start(LWX, lru_wx[0].rearrange("b i j -> i b j")).then_inc(E("lwx"), 16)
            if stop:
                sp.wait_ge(E("stop"), 1)
                sp.wait_ge(E("rout_in"), 32)
                sp.wait_ge(E("b2_in"), 16)
                for name, dst in dump.items():
                    sp.dma_start(dst, locals_[name]).then_inc(E("dumped"), 16)
                sp.wait_ge(E("dumped"), 16 * len(dump))
                return
            sp.wait_ge(E("mix_done"), 1)
            sp.wait_ge(E("mix_done_pe"), 1)

            def load_expert(e, item, first):
                for c in range(KD):
                    if not first:
                        sp.wait_ge(E("w1_used"), (item - 1) * KD + c + 1)
                    sp.dma_start(W1[:, c, :], exp_w1[0, bass.ds(e, 1), c * P:(c + 1) * P, :]
                                 .rearrange("e p n -> p (e n)")).then_inc(E(f"w1_in{c}"), 16)
                for c in range(KF // 2):
                    if not first:
                        sp.wait_ge(E("w2_used"), (item - 1) * (KF // 2) + c + 1)
                    sp.dma_start(W2[:, 2 * c:2 * c + 2, :],
                                 exp_w2[0, bass.ds(e, 1), 2 * c * P:(2 * c + 2) * P, :]
                                 .rearrange("e (c p) n -> p (e c) n", p=P)
                                 ).then_inc(E(f"w2_in{c}"), 16)
            load_expert(0, 0, True)
            with sp.Fori(1, NE) as e:
                load_expert(e, e, False)
            sp.wait_ge(E("rounds_ready"), 1)
            rounds = sp.value_load(NR[0:1, 0:1], min_val=1, max_val=ROUNDS)
            with sp.If(rounds > 1):
                with sp.Fori(1, rounds) as r:
                    with sp.Fori(0, NE) as e:
                        load_expert(e, r * NE + e, False)
            sp.wait_ge(E("out_ready"), 1)
            sp.dma_start(out[0].rearrange("(t p) d -> p t d", p=P), X1).then_inc(E("stored"), 16)
            sp.wait_ge(E("stored"), 16)

        @block.gpsimd
        def _(gp):
            cleared = [0]

            def clear(region, value, event):
                cleared[0] += 1
                nc_g.memset(region, value).then_inc(E("cleared"), 1)
                gp.wait_ge(E("cleared"), cleared[0])
                gp.sem_inc(E(event), 1)
            clear(BIAS, 0.0, "small_zero")
            clear(ALOG, 0.0, "small_zero")
            clear(VR, 0.0, "small_zero")
            clear(WSM, 0.0, "small_zero")
            clear(GIN[:, :, 0:3], 0.0, "gin_pad")
            clear(LX[:, :, 0:3], 0.0, "lx_pad")
            clear(RX, 0.0, "rx_zero")
            clear(NM, 0.0, "nm_zero")
            clear(QM[64:128, :, 0, :], 0.0, "qm_zero")
            clear(QM[0:64, :, 1, :], 0.0, "qm_zero")
            clear(V1[:, :, :, 128:129], 1.0, "v1_one")
            gp.wait_ge(E("gsilu"), 1)
            for R in (QB, KB):
                clear(R[64:128, :, 0, :], 0.0, "qb_zero")
                clear(R[0:64, :, 1, :], 0.0, "qb_zero")

        @block.tensor
        def _(pe):
            mm = nc.tensor.matmul

            def take(name):
                bank, n = uses[name]
                if n > 1:
                    pe.wait_ge(E(f"bank_free{bank}"), n - 1)
                return PS[:, bank, :]

            def done(name, ins):
                ins.then_inc(E(f"bank_full{uses[name][0]}"), 1)

            def weights(name):
                n = stream_at[name]
                pe.wait_ge(E(f"w_in{n % WBUFS}"), 16 * (n // WBUFS + 1))
                return WB[n % WBUFS]

            def proj(name, rhs=XT, nk=KD):
                w = weights(name)
                o = take(name)
                for m in range(2):
                    for c in range(nk):
                        ins = mm(o[:, m * S:(m + 1) * S], w[:, c, m * P:(m + 1) * P], rhs[:, c, :],
                                 start=(m == 0 and c == 0), stop=(c == nk - 1), skip_group_check=True)
                done(name, ins)

            def proj_tok(name, lhs, nk=KD):
                w = weights(name)
                o = take(name)
                for t in range(NT):
                    for c in range(nk):
                        ins = mm(o[:, t * GW:(t + 1) * GW], lhs[:, c, t * P:(t + 1) * P], w[:, c, :],
                                 start=(t == 0 and c == 0), stop=(c == nk - 1), skip_group_check=True)
                done(name, ins)

            def many(name, parts):
                o = take(name)
                for n, (lo, hi, lhs, rhs) in enumerate(parts):
                    ins = mm(o[0:lhs.shape[-1], lo:hi], lhs, rhs, start=True, stop=True,
                             skip_group_check=True)
                done(name, ins)

            pe.wait_ge(E("planes_in"), 16)
            pe.wait_ge(E("x_in"), 16)
            for n in range(4):
                many(f"xT{n}", [(m * S + t * P, m * S + t * P + P, XTOK[:, t, (2 * n + m) * P:(2 * n + m + 1) * P],
                                 ident) for m in range(2) for t in range(NT)])
            pe.wait_ge(E("vec_in"), 16 * 9)
            many("vec", [(0, P, VR, ident)])
            [moved(pe, f"xT{n}") for n in range(4)]
            pe.wait_ge(E("wsm_in"), 16 * 4)
            o = take("small")
            for c in range(KD):
                ins = mm(o[:, 0:S], WSM[:, c, :], XT[:, c, :], start=(c == 0), stop=(c == KD - 1))
            done("small", ins)
            for n in range(6):
                proj(f"gq{n}")
            for n in range(4):
                proj(f"lx{n}")
            pe.wait_ge(E("rows_ready"), 1)
            pe.wait_ge(E("rows_ready_act"), 3)
            many("rc", [(t * S + k * P, t * S + k * P + P, r[:, t * P:(t + 1) * P], ident)
                        for t in range(NT) for k, r in enumerate((RW, RX))])
            for n in range(4):
                pe.wait_ge(E("squares"), n // 2 + 1)
                many(f"ss{n}", [(0, 512, CM[:, K_BLK], SQ[:, 2 * n:2 * n + 2, :])])
            for n in range(2):
                o = take(f"bb{n}")
                for m in range(2):
                    for a in range(2):
                        ins = mm(o[64 * a:64 * a + 64, m * S:m * S + S],
                                 ident[:, 96 + 4 * n + 2 * m + a:97 + 4 * n + 2 * m + a].to_broadcast([P, 64]),
                                 RW, start=True, stop=True, skip_group_check=True)
                done(f"bb{n}", ins)
            for n in range(2):
                o = take(f"gb{n}")
                for m in range(2):
                    for a in range(2):
                        ins = mm(o[64 * a:64 * a + 64, m * S:m * S + S],
                                 ident[:, 64 + 4 * n + 2 * m + a:65 + 4 * n + 2 * m + a].to_broadcast([P, 64]),
                                 RW, start=True, stop=True, skip_group_check=True)
                done(f"gb{n}", ins)
            pe.wait_ge(E("gsilu_v"), 1)
            for t in range(NT):
                many(f"vt{t}", [(j * P, j * P + P, GCO[:, 8 + j, t * P:(t + 1) * P], ident) for j in range(GP)])
            pe.wait_ge(E("khat"), 1)
            for t in range(NT):
                many(f"kt{t}", [(j * P, j * P + P, KT[:, j, t * P:(t + 1) * P], ident) for j in range(GP)])
            for n in range(4):
                many(f"gr{n}", [(m * S, m * S + S, ident[:, 64 + 2 * n + m:65 + 2 * n + m].to_broadcast([P, P]), RW)
                                for m in range(2)])
            pe.wait_ge(E("kb_ready"), 1)
            for name, R in (("at", KB), ("pt", QB)):
                for n in range(4):
                    t = n // 2
                    many(f"{name}{n}", [(m * S, m * S + S, KT[:, 2 * (n % 2) + m, t * P:(t + 1) * P],
                                         R[:, 2 * (n % 2) + m, :, t * P:(t + 1) * P]) for m in range(2)])
            for n in range(4):
                pe.wait_ge(E("xt1"), n + 1)
                many(f"x1{n}", [(q * P, q * P + P, XTi[:, n, q * P:(q + 1) * P], ident) for q in range(4)])
            filler = [f"ly{n}" for n in range(4)] + ["mq", "mk", "mv0", "mv1", "mo0", "mo1"]

            def fill(name):
                if name[:2] == "mv":
                    proj_tok(name, XT)
                else:
                    proj(name)
            for k in range(1, 6):
                for n in range(4):
                    moved(pe, f"x1{n}" if k == 1 else f"t{k - 1}{n}")
                    many(f"y{k}{n}", [(q * P, q * P + P, AT[:, n, q * P:(q + 1) * P], X_[:, n, q * P:(q + 1) * P])
                                      for q in range(4)])
                fill(filler[2 * k - 2])
                if k < 5:
                    for n in range(4):
                        moved(pe, f"y{k}{n}")
                        many(f"z{k}{n}", [(q * P, q * P + P, XTi[:, n, q * P:(q + 1) * P],
                                           Y_[:, n, q * P:(q + 1) * P]) for q in range(4)])
                for n in range(4):
                    moved(pe, f"y{k}{n}")
                    many(f"t{k}{n}", [(q * P, q * P + P, Y_[:, n, q * P:(q + 1) * P],
                                       XTi[:, n, q * P:(q + 1) * P]) for q in range(4)])
                fill(filler[2 * k - 1])
            [moved(pe, f"t5{n}") for n in range(4)]
            for t in range(NT):
                many(f"u{t}", [(h * GK, h * GK + GK, XTi[:, 2 * t + h // 4, (h % 4) * P:(h % 4 + 1) * P],
                                BV[:, t, h * GK:(h + 1) * GK]) for h in range(GH)])
            for t in range(NT):
                o = take(f"w{t}")
                for h in range(GH):
                    a = 64 * (h % 2)
                    ins = mm(o[a:a + 64, (h // 2) * P:(h // 2 + 1) * P], KBE[:, t, h * GK:(h + 1) * GK],
                             XTi[:, 2 * t + h // 4, (h % 4) * P:(h % 4 + 1) * P], start=True, stop=True,
                             skip_group_check=True)
                done(f"w{t}", ins)
            proj("gz0")
            proj("gz1")
            pe.wait_ge(E("lwa"), 16)
            pe.wait_ge(E("lwx"), 16)
            pe.wait_ge(E("xa_ready"), 1)
            for c in range(NC):
                t, a = c // 2, 64 * (c % 2)
                pe.wait_ge(E("state"), c + 1)
                moved(pe, f"w{t}")
                o = take(f"ws{c}")
                for j in range(GP):
                    ins = mm(o[a:a + 64, j * P:(j + 1) * P], WT[:, t, j, a:a + 64], ST[:, j * P:(j + 1) * P],
                             start=True, stop=True, skip_group_check=True)
                done(f"ws{c}", ins)
                for b in (2 * c, 2 * c + 1):
                    many(f"lg{b}", [(0, S, LWA[:, b, :], XA[:, b, :]), (S, 2 * S, LWX[:, b, :], XA[:, b, :])])
                oo = take(f"o{t}") if c % 2 == 0 else ps(f"o{t}")
                for j in range(GP):
                    mm(oo[a:a + 64, j * P:(j + 1) * P], QG[:, j, c * CH:(c + 1) * CH], ST[:, j * P:(j + 1) * P],
                       start=(j == 0), stop=False, skip_group_check=True)
                moved(pe, f"ws{c}")
                o = take(f"sn{c}")
                for j in range(GP):
                    ins = mm(o[:, j * P:(j + 1) * P], KDE[a:a + 64, t, j * P:(j + 1) * P],
                             DE[a:a + 64, t, j * P:(j + 1) * P], start=True, stop=True, skip_group_check=True)
                done(f"sn{c}", ins)
                for h in range(GH):
                    q = (h % 4) * P + a
                    ins = mm(oo[a:a + 64, h * GK:(h + 1) * GK], PT[a:a + 64, 2 * t + h // 4, q:q + 64],
                             DE[a:a + 64, t, h * GK:(h + 1) * GK], start=False, stop=True, skip_group_check=True)
                if c % 2 == 1:
                    done(f"o{t}", ins)
            for t in range(NT):
                pe.wait_ge(E("o_norm"), t + 1)
                many(f"ot{t}", [(j * P, j * P + P, OQ[:, t, j * P:(j + 1) * P], ident) for j in range(GP)])
            for n in range(2):
                many(f"mr{n}", [(m * S, m * S + S, ident[:, 2 * n + m:2 * n + m + 1].to_broadcast([P, P]), NM)
                                for m in range(2)])
            for j in range(2):
                many(f"ms{j}0", [(0, 512, MK[:, j, 0:P], QM[:, j, :, :])])
            for j in range(2):
                many(f"ms{j}1", [(0, 256, MK[:, j, P:2 * P], QM[:, j, :, P:2 * P])])
            pe.wait_ge(E("ms_ready"), 2)
            for t in range(NT):
                for j in range(2):
                    o = take(f"mn{t}{j}")
                    for a in range(2):
                        h = 2 * j + a
                        blocks = [(0, 0)] if t == 0 else [(1, 0), (2, 1)]
                        for n, (b, s) in enumerate(blocks):
                            ins = mm(o[:, a * 129:a * 129 + 129], MS[:, h, b, :], V1[:, s, h, :],
                                     start=(n == 0 and a == 0), stop=(n == len(blocks) - 1),
                                     skip_group_check=True)
                    done(f"mn{t}{j}", ins)
            for t in range(NT):
                pe.wait_ge(E("mn_norm"), t + 1)
                many(f"mt{t}", [(h * P, h * P + P, MQ2[:, t, h, :], ident) for h in range(MH)])
            for n, (h, nk, ev) in enumerate(((LY, 8, "ha_ready"), (HB, 4, "hb_ready"), (HC, 4, "hc_ready"))):
                for d in range(4):
                    proj(f"ga{n}{d}")
                    if d == 0:
                        pe.wait_ge(E(ev), 1)
                    proj(f"br{n}{d}", h, nk)
            pe.wait_ge(E("merged"), 1)
            for d in range(4):
                proj_tok(f"wo{d}", MG)
            if stop:
                return
            pe.wait_ge(E("x1_ready"), 1)
            for n in range(4):
                many(f"x1T{n}", [(m * S + t * P, m * S + t * P + P, X1[:, t, (2 * n + m) * P:(2 * n + m + 1) * P],
                                  ident) for m in range(2) for t in range(NT)])
            pe.wait_ge(E("b1r_in"), 16)
            [moved(pe, f"x1T{n}") for n in range(4)]
            o = take("lgt")
            for t in range(NT):
                for c in range(KD):
                    ins = mm(o[:, t * NE:(t + 1) * NE], X1T[:, c, t * P:(t + 1) * P], ROUT[:, c, :],
                             start=(c == 0 and t == 0), stop=(c == KD - 1), skip_group_check=True)
            done("lgt", ins)
            pe.wait_ge(E("sel_ready"), 1)
            o = take("cnt")
            mm(o[:, 0:32], CM[:, K_BEFORE], SEL[:, 0, :], start=True, stop=True, skip_group_check=True)
            mm(o[:, 32:64], CM[:, K_BEFORE], SEL[:, 1, :], start=False, stop=False, skip_group_check=True)
            mm(o[:, 32:64], CM[:, K_ONES], SEL[:, 0, :], start=False, stop=True, skip_group_check=True)
            mm(o[:, 64:96], CM[:, K_ONES], SEL[:, 0, :], start=False, stop=False, skip_group_check=True)
            ins = mm(o[:, 64:96], CM[:, K_ONES], SEL[:, 1, :], start=False, stop=True, skip_group_check=True)
            done("cnt", ins)
            pe.wait_ge(E("gates_ready"), 1)
            o = take("gT")
            for t in range(NT):
                ins = mm(o[0:NE, t * P:(t + 1) * P], GAT[:, t, 0:NE], ident, start=True, stop=True,
                         skip_group_check=True)
            done("gT", ins)
            for b in range(4, 8):
                pe.wait_ge(E(f"bank_free{b}"), bank_total[b])
            pe.wait_ge(E("gT_ready"), 1)
            for t in range(NT):
                for h in range(2):
                    mm(PS[:, 4 + 2 * t + h, :], GTT[0:NE, t * P:(t + 1) * P], B2[0:NE, h * 512:(h + 1) * 512],
                       start=True, stop=False, skip_group_check=True)

            def scatter():
                for t in range(NT):
                    for a in range(2):
                        ins = mm(PS[:, 4 + 2 * t + a, :], GTS[64 * a:64 * a + CAP, t * P:(t + 1) * P],
                                 YS[64 * a:64 * a + CAP, :], start=False, stop=False, skip_group_check=True)
                return ins

            def gather():
                for t in range(NT):
                    for a in range(2):
                        ins = mm(PS[64 * a:64 * a + CAP, 2, :], ONE[:, t, :], X1[:, t, a * 512:(a + 1) * 512],
                                 start=(t == 0), stop=(t == NT - 1), skip_group_check=True)
                return ins

            def turn(bank, src):
                for q in range(4):
                    ins = mm(PS[:, bank, q * P:(q + 1) * P], src[:, q * P:(q + 1) * P], ident,
                             start=True, stop=True, skip_group_check=True)
                return ins

            for b in range(4):
                pe.wait_ge(E(f"bank_free{b}"), bank_total[b])
            pe.wait_ge(E("onehot"), 1)
            gather().then_inc(E("xg_full"), 1)
            pe.wait_ge(E("xg_ready"), 1)
            turn(2, XG).then_inc(E("xe_full"), 1)
            rounds = pe.value_load(NR[0:1, 0:1], min_val=1, max_val=ROUNDS)
            with pe.Fori(0, rounds) as r, pe.Fori(0, NE) as e:
                i = r * NE + e
                pe.wait_ge(E("xe_ready"), i + 1)
                pe.wait_ge(E("pick"), i + 1)
                for b in range(2):
                    for a in range(2):
                        mm(PS[64 * a:64 * a + CAP, b, :], PICK[0:NE, :],
                           B1R[0:NE, b * FF + a * 512:b * FF + a * 512 + 512], start=True, stop=False,
                           skip_group_check=True)
                for c in range(KD):
                    pe.wait_ge(E(f"w1_in{c}"), 16 * i + 16)
                    for b in range(2):
                        for a in range(2):
                            ins = mm(PS[64 * a:64 * a + CAP, b, :], XE[:, c % 4, 64 * (c // 4):64 * (c // 4) + CAP],
                                     W1[:, c, b * FF + a * 512:b * FF + a * 512 + 512], start=False,
                                     stop=(c == KD - 1), skip_group_check=True)
                    ins.then_inc(E("w1_used"), 1)
                pe.wait_ge(E("ys_ready"), i + 1)
                scatter().then_inc(E("scattered"), 1)
                pe.wait_ge(E("onehot"), i + 2)
                gather().then_inc(E("xg_full"), 1)
                pe.wait_ge(E("gated"), i + 1)
                for t in range(NT):
                    ins = mm(PS[:, 3, t * P:(t + 1) * P], GAD[:, t, :], ident, start=True, stop=True,
                             skip_group_check=True)
                ins.then_inc(E("gt_full"), 1)
                pe.wait_ge(E("xg_ready"), i + 2)
                turn(2, XG).then_inc(E("xe_full"), 1)
                pe.wait_ge(E("gt_ready"), i + 1)
                pe.wait_ge(E("hid_ready"), i + 1)
                turn(3, HID).then_inc(E("ht_full"), 1)
                pe.wait_ge(E("ht_ready"), i + 1)
                for c in range(KF):
                    if c % 2 == 0:
                        pe.wait_ge(E(f"w2_in{c // 2}"), 16 * i + 16)
                    for a in range(2):
                        ins = mm(PS[64 * a:64 * a + CAP, 3, :], HT[:, c % 4, 64 * (c // 4):64 * (c // 4) + CAP],
                                 W2[:, c, a * 512:(a + 1) * 512], start=(c == 0), stop=(c == KF - 1),
                                 skip_group_check=True)
                    if c % 2:
                        ins.then_inc(E("w2_used"), 1)
            pe.wait_ge(E("ys_ready"), rounds * NE + 1)
            scatter().then_inc(E("acc_done"), 1)

        @block.scalar
        def _(act):
            tick = [0]

            def step(ins):
                tick[0] += 1
                ins.then_inc(E("act_own"), 1)
                act.wait_ge(E("act_own"), tick[0])

            A = nc_s.activation
            act.dma_start(CM, planes.rearrange("p (k n) -> p k n", n=P)).then_inc(E("planes_in"), 16)
            act.wait_ge(E("small_zero"), 4)
            v = VR
            for row, src in ((V_CW, lru_conv_w[0].rearrange("w (b p) -> (w b) p", p=P)),
                             (V_CB, lru_conv_b[0].rearrange("(b p) -> b p", p=P)),
                             (V_BA, lru_ba[0]), (V_BX, lru_bx[0]),
                             (V_LAM, lru_lambda[0].rearrange("(b p) -> b p", p=P)),
                             (V_GCW, gd_conv_w[0].rearrange("w (b p) -> (w b) p", p=P)),
                             (V_MG, ml_norm_g[0])):
                act.dma_start(v[row:row + src.shape[0], :], src).then_inc(E("vec_in"), 16)
            for a in range(2):
                act.dma_start(v[V_GG:V_GG + 1, 64 * a:64 * a + 64], gd_norm_g[0:1, :]).then_inc(E("vec_in"), 16)
            for q, (col, n) in enumerate(((C_MI, MH), (C_MI + MH, MH), (C_GA, GH), (C_GA + GH, GH))):
                act.dma_start(WSM[:, :, 32 * q:32 * q + n], w_in[0, :, col:col + n]
                              .rearrange("(c p) n -> p c n", p=P)).then_inc(E("wsm_in"), 16)
            for row, dst, src in ((0, BIAS, ml_i_bias), (32, BIAS, ml_f_bias), (64, BIAS, gd_dt_bias),
                                  (64, ALOG, gd_a_log)):
                n = src.shape[1]
                act.dma_start(dst[row:row + n, :], src.rearrange("a n -> n a")).then_inc(E("bias_in"), 16)
            act.dma_start(ROUT, router_w[0].rearrange("(c p) e -> p c e", p=P)).then_inc(E("rout_in"), 16)
            act.dma_start(RBIAS, router_b[0].partition_broadcast(P)).then_inc(E("rout_in"), 16)
            act.dma_start(B2[0:NE, :], exp_b2[0]).then_inc(E("b2_in"), 16)
            for n in range(4):
                full(act, f"xT{n}")
                nc_s.copy(XT[:, 2 * n:2 * n + 2, :], ps(f"xT{n}").rearrange("p (c s) -> p c s", s=S)
                          ).then_inc(free(f"xT{n}"), 1)

            full(act, "vec")
            nc_s.copy(VC, ps("vec")[:, 0:P]).then_inc(free("vec"), 1)

            act.wait_ge(E("bias_in"), 64)
            step(A(ALOG, ALOG, ACT.Exp))
            nc_s.mul(COEF, ALOG, CM[:, K_COLS, 1:2]).then_inc(E("coef"), 1)
            moved(act, "vec")
            A(TS[:, 0:8], VC[:, V_LAM:V_LAM + 8], ACT.Abs).then_inc(E("lam_abs"), 1)
            act.wait_ge(E("lam_abs"), 1)
            A(TS[:, 0:8], TS[:, 0:8], ACT.Exp, scale=-1.0).then_inc(E("lam_exp"), 1)

            def evac(name, dst, n=0, func=None):
                full(act, name)
                src = ps(name).rearrange("p (c s) -> p c s", s=S)
                if func is None:
                    ins = nc_s.copy(dst, src)
                else:
                    ins = A(dst, src, func)
                ins.then_inc(free(name), 1)

            act.wait_ge(E("gin_pad"), 1)
            for n in range(6):
                evac(f"gq{n}", GIN[:, 2 * n:2 * n + 2, 3:])
                if n == 0:
                    act.wait_ge(E("row_abs"), 1)
                    A(ROWT[3], ROWT[2], ACT.Exp, scale=-1.0).then_inc(E("row_exp"), 1)
            act.wait_ge(E("lx_pad"), 1)
            for n in range(2):
                evac(f"lx{n}", LX[:, 2 * n:2 * n + 2, 3:])
            act.wait_ge(E("row_scan"), 1)
            nc_s.copy(ROWT[7][0:32], RB[32:64]).then_inc(E("row_b0"), 1)
            nc_s.copy(RW[64:96], RB[64:96]).then_inc(E("rows_ready_act"), 1)
            act.wait_ge(E("row_mb"), 1)
            A(RW[32:64], ROWT[6][0:32], ACT.Exp, scale=-1.0).then_inc(E("rows_ready_act"), 1)
            act.wait_ge(E("rx_zero"), 1)
            act.wait_ge(E("row_kd"), 1)
            A(RX[64:96], ROWT[5][64:96], ACT.Exp).then_inc(E("rows_ready_act"), 1)
            for n in range(2, 4):
                evac(f"lx{n}", LX[:, 2 * n:2 * n + 2, 3:])
            A(RW[96:128], ROWT[0][96:128], ACT.Sigmoid).then_inc(E("rows_beta"), 1)
            for n in range(3):
                act.wait_ge(E("gconv"), n + 1)
                A(GSIG[:, 4 * n:4 * n + 4, :], GCO[:, 4 * n:4 * n + 4, :], ACT.Sigmoid).then_inc(E("gsig"), 1)
            for n in range(2):
                act.wait_ge(E("gsilu_qk"), n + 1)
                A(SQ[:, 4 * n:4 * n + 4, :], GCO[:, 4 * n:4 * n + 4, :], ACT.Square).then_inc(E("squares"), 1)
            act.wait_ge(E("eps_ready"), 1)
            full(act, "rc")
            nc_s.copy(RC, ps("rc").rearrange("p (t k n) -> p t k n", t=2, k=2)).then_inc(free("rc"), 1)

            for n in range(4):
                full(act, f"ss{n}")
                A(RN[:, 2 * n:2 * n + 2, :], ps(f"ss{n}").rearrange("p (c s) -> p c s", s=S), ACT.Sqrt,
                  bias=TS[:, 31:32]).then_inc(free(f"ss{n}"), 1)

            for n in range(2):
                full(act, f"gb{n}")
                A(EG[:, 2 * n:2 * n + 2, :], ps(f"gb{n}").rearrange("p (c s) -> p c s", s=S), ACT.Exp
                  ).then_inc(free(f"gb{n}"), 1)

            moved(act, "rc")
            A(TS[:, 8:24].rearrange("p (t h) -> p t h", t=NT), RC[:, :, 0, 64:72], ACT.Exp).then_inc(E("egc"), 1)
            for n in range(4):
                act.wait_ge(E("gam_arg"), n + 1)
                A(GAM[:, n, :], GAM[:, n, :], ACT.Exp).then_inc(E("gam"), 1)
            for n in range(4):
                full(act, f"x1{n}")
                nc_s.copy(X_[:, n, :], ps(f"x1{n}")).then_inc(free(f"x1{n}"), 1)

            for n in range(4):
                evac(f"ly{n}", LY[:, 2 * n:2 * n + 2, :])
            act.wait_ge(E("qm_zero"), 2)
            full(act, "mq")
            nc_s.mul(QM[0:64, :, 0, :], ps("mq")[0:64].rearrange("p (c s) -> p c s", s=S), MQ ** -0.5)
            nc_s.mul(QM[64:128, :, 1, :], ps("mq")[64:128].rearrange("p (c s) -> p c s", s=S), MQ ** -0.5
                     ).then_inc(free("mq"), 1)
            evac("mk", MK)
            act.wait_ge(E("v1_one"), 1)
            for n in range(2):
                full(act, f"mv{n}")
                nc_s.copy(V1[:, :, 2 * n:2 * n + 2, 0:128],
                          ps(f"mv{n}").rearrange("p (t h e) -> p t h e", t=NT, h=2)).then_inc(free(f"mv{n}"), 1)
                act.wait_ge(free(f"mv{n}"), uses[f"mv{n}"][1])
            for n in range(2):
                evac(f"mo{n}", MO[:, 2 * n:2 * n + 2, :], func=ACT.Sigmoid)
            for t in range(NT):
                full(act, f"u{t}")
                nc_s.copy(U_[:, t, :], ps(f"u{t}")).then_inc(free(f"u{t}"), 1)

            for t in range(NT):
                full(act, f"w{t}")
                nc_s.copy(WT[:, t, :, :], ps(f"w{t}").rearrange("p (j n) -> p j n", j=GP)).then_inc(free(f"w{t}"), 1)

            for n in range(2):
                full(act, f"gz{n}")
                nc_s.copy(GZ[:, 2 * n:2 * n + 2, :], ps(f"gz{n}").rearrange("p (c s) -> p c s", s=S)
                          ).then_inc(free(f"gz{n}"), 1)
                act.wait_ge(free(f"gz{n}"), uses[f"gz{n}"][1])
            act.wait_ge(E("lx_free"), 1)
            A(LT[:, 0:4, :], GZ, ACT.Sigmoid).then_inc(E("zsig"), 1)
            act.wait_ge(E("xt_free"), 1)
            
            for b in range(NB):
                full(act, f"lg{b}")
                A(LR[:, b, :], ps(f"lg{b}")[:, 0:S], ACT.Sigmoid, bias=VC[:, V_BA + b:V_BA + b + 1])
                A(LG[:, b, :], ps(f"lg{b}")[:, S:2 * S], ACT.Sigmoid, bias=VC[:, V_BX + b:V_BX + b + 1]
                  ).then_inc(free(f"lg{b}"), 1)
            act.wait_ge(free("lg7"), uses["lg7"][1])
            act.wait_ge(free("lg6"), uses["lg6"][1])
            act.sem_inc(E("lgates"), 1)
            act.wait_ge(E("lsp"), 1)
            for b in range(NB):
                A(LA[:, b, :], LR[:, b, :], ACT.Exp, scale=NLSP[:, b:b + 1])
                ins = A(LU[:, b, :], LR[:, b, :], ACT.Tanh, scale=LSP[:, b:b + 1])
            ins.then_inc(E("la"), 1)
            for t in range(NT):
                act.wait_ge(E("oss"), t + 1)
                A(TS[:, 8 * t:8 * t + 8], TS[:, 8 * t:8 * t + 8], ACT.Sqrt, bias=TS[:, 31:32], scale=1.0 / GK
                  ).then_inc(E("osq"), 1)
            for n in range(2):
                act.wait_ge(E("me_arg"), n + 1)
                A(ME[:, 2 * n:2 * n + 2, :, :], ME[:, 2 * n:2 * n + 2, :, :], ACT.Exp).then_inc(E("me"), 1)
            for t in range(NT):
                act.wait_ge(E("mn_scaled"), t + 1)
                for h in range(MH):
                    ins = A(MQ2[:, t, h, :], MN[:, t, h, :], ACT.Square,
                            accum_out=RT2[:, 4 * t + h:4 * t + h + 1])
                ins.then_inc(E("mss"), 1)
                act.wait_ge(E("mss"), 2 * t + 1)
                A(RT2[:, 8 + 4 * t:12 + 4 * t], RT2[:, 4 * t:4 * t + 4], ACT.Sqrt, bias=TS[:, 31:32],
                  scale=1.0 / MV).then_inc(E("mss"), 1)
            act.wait_ge(E("gelu_arg"), 1)
            act.wait_ge(E("la"), 1)
            A(LR, LR, ACT.Tanh, scale=0.7978845608028654).then_inc(E("gelu_tanh"), 1)
            act.wait_ge(E("lu_arg"), 1)
            A(LU, LU, ACT.Sqrt, scale=2.0).then_inc(E("lu"), 1)
            for n in range(3):
                for d in range(4):
                    k = 4 * n + d
                    full(act, f"ga{n}{d}")
                    if k >= 2:
                        moved(act, f"br{(k - 2) // 4}{(k - 2) % 4}")
                    A(SG[k % 2], ps(f"ga{n}{d}"), ACT.Sigmoid).then_inc(free(f"ga{n}{d}"), 1)

            if stop:
                return
            act.wait_ge(E("merged"), 1)
            act.dma_start(LNG, ln1_g[0].partition_broadcast(P)).then_inc(E("ln1_in"), 16)
            act.dma_start(LNB, ln1_b[0].partition_broadcast(P)).then_inc(E("ln1_in"), 16)
            act.dma_start(B1R[0:NE, :], exp_b1[0]).then_inc(E("b1r_in"), 16)
            act.wait_ge(E("ln1_var"), 1)
            A(TS[:, 8:10], TS[:, 8:10], ACT.Sqrt, bias=TS[:, 30:31]).then_inc(E("ln1_sd"), 1)
            for n in range(4):
                full(act, f"x1T{n}")
                nc_s.copy(X1T[:, 2 * n:2 * n + 2, :], ps(f"x1T{n}").rearrange("p (c s) -> p c s", s=S)
                          ).then_inc(free(f"x1T{n}"), 1)


            act.wait_ge(E("exl_arg"), 1)
            A(EXL, EXL, ACT.Exp).then_inc(E("exl"), 1)
            full(act, "gT")
            nc_s.copy(GTT[0:NE, :], ps("gT")[0:NE, 0:S]).then_inc(free("gT"), 1)
            act.wait_ge(free("gT"), uses["gT"][1])
            act.wait_ge(E("b2_in"), 16)
            act.sem_inc(E("gT_ready"), 1)
            act.wait_ge(E("x1_ready"), 1)
            act.dma_start(LNG, ln2_g[0].partition_broadcast(P)).then_inc(E("ln2_in"), 16)
            act.dma_start(LNB, ln2_b[0].partition_broadcast(P)).then_inc(E("ln2_in"), 16)
            act.wait_ge(E("xg_full"), 1)
            nc_s.copy(XG, PS[:, 2, :]).then_inc(E("xg_ready"), 1)
            act.wait_ge(E("xe_full"), 1)
            nc_s.copy(XE, PS[:, 2, :].rearrange("p (q n) -> p q n", q=4)).then_inc(E("xe_ready"), 1)
            rounds = act.value_load(NR[0:1, 0:1], min_val=1, max_val=ROUNDS)
            with act.Fori(0, rounds) as r, act.Fori(0, NE) as e:
                i = r * NE + e
                act.wait_ge(E("glu_ready"), i + 1)
                A(SIG, GLU, ACT.Sigmoid, scale=SWIGLU).then_inc(E("sig_ready"), 1)
                act.wait_ge(E("xg_full"), i + 2)
                nc_s.copy(XG, PS[:, 2, :]).then_inc(E("xg_ready"), 1)
                act.wait_ge(E("gt_full"), i + 1)
                nc_s.copy(GTS, PS[:, 3, 0:S]).then_inc(E("gt_ready"), 1)
                act.wait_ge(E("xe_full"), i + 2)
                nc_s.copy(XE, PS[:, 2, :].rearrange("p (q n) -> p q n", q=4)).then_inc(E("xe_ready"), 1)
                act.wait_ge(E("w2_used"), (KF // 2) * i + KF // 2)
                nc_s.copy(YS, PS[:, 3, :]).then_inc(E("ys_ready"), 1)
            act.wait_ge(E("ln2_var"), 1)
            A(TS[:, 8:10], TS[:, 8:10], ACT.Sqrt, bias=TS[:, 30:31]).then_inc(E("ln2_sd"), 1)

        @block.vector
        def _(dve):
            tick = [0]

            def step(ins):
                tick[0] += 1
                ins.then_inc(E("dve_own"), 1)
                dve.wait_ge(E("dve_own"), tick[0])

            tt, ts, stt = nc_v.tensor_tensor, nc_v.tensor_scalar, nc_v.scalar_tensor_tensor

            def softplus_tail(y, e, out, t1, t2, t3):
                step(ts(t1, e, 2.0, None, ALU.add))
                step(nc_v.reciprocal(t1, t1))
                step(tt(t1, t1, e, ALU.mult))
                step(tt(t2, t1, t1, ALU.mult))
                step(ts(t3, t2, 1.0 / 15, None, ALU.mult))
                for n in (13, 11, 9, 7, 5, 3):
                    step(stt(t3, t3, 1.0 / n, t2, ALU.add, ALU.mult))
                step(stt(t3, t3, 1.0, t1, ALU.add, ALU.mult))
                step(ts(t1, y, 0.0, None, ALU.max))
                step(stt(out, t3, 2.0, t1, ALU.mult, ALU.add))

            dve.wait_ge(E("planes_in"), 16)
            nc_v.memset(TS[:, 31:32], RMS_EPS).then_inc(E("eps_ready"), 1)
            nc_v.memset(TS[:, 30:31], LN_EPS).then_inc(E("eps2_ready"), 1)
            moved(dve, "vec")
            dve.wait_ge(E("lam_exp"), 1)
            step(ts(TS[:, 8:16], VC[:, V_LAM:V_LAM + 8], -1.0, None, ALU.mult))
            softplus_tail(TS[:, 8:16], TS[:, 0:8], TS[:, 0:8], TS[:, 16:24], LSP, NLSP)
            step(ts(LSP, TS[:, 0:8], LRU_C, None, ALU.mult))
            ts(NLSP, TS[:, 0:8], -LRU_C, None, ALU.mult).then_inc(E("lsp"), 1)
            full(dve, "small")
            dve.wait_ge(E("bias_in"), 64)
            dve.wait_ge(E("coef"), 1)
            PRE, YR, AB, EX, SPT, L2, MB, B0 = ROWT
            ts(PRE, ps("small")[:, 0:S], BIAS, None, ALU.add).then_inc(free("small"), 1)
            dve.wait_ge(free("small"), 1)
            step(ts(YR, PRE, CM[:, K_COLS, 0:1], None, ALU.mult))
            stt(AB, YR, -1.0, YR, ALU.mult, ALU.max).then_inc(E("row_abs"), 1)
            dve.wait_ge(E("row_exp"), 1)
            softplus_tail(YR, EX, SPT, L2, MB, B0)
            step(ts(SPT, SPT, COEF, None, ALU.mult))
            nc_v.tensor_tensor_scan(RB, CM[:, K_RST0:K_RST1 + 1, :].rearrange("p a b -> p (a b)"), SPT, 0.0,
                                    ALU.mult, ALU.add).then_inc(E("row_scan"), 1)
            dve.wait_ge(E("row_scan"), 1)
            dve.wait_ge(E("row_b0"), 1)
            step(tt(RW[0:32], PRE[0:32], B0[0:32], ALU.subtract))
            step(nc_v.tensor_tensor_scan(SPT[0:32], RW[0:32], RW[0:32], 0.0, ALU.max, ALU.max))
            tt(MB[0:32], SPT[0:32], B0[0:32], ALU.add).then_inc(E("row_mb"), 1)
            dve.wait_ge(E("nm_zero"), 1)
            step(ts(NM[0:32], SPT[0:32], -1.0, None, ALU.mult))
            g4 = RB[64:96].rearrange("p (c l) -> p c l", l=CH)
            tt(L2[64:96].rearrange("p (c l) -> p c l", l=CH), g4[:, :, CH - 1:CH].to_broadcast([32, NC, CH]), g4,
               ALU.subtract).then_inc(E("row_kd"), 1)
            dve.wait_ge(E("row_kd"), 1)
            dve.wait_ge(E("rows_beta"), 1)
            dve.sem_inc(E("rows_ready"), 1)

            def conv(dst, src, w0, nb, b, bias=None):
                taps = [VC[:, w0 + nb * j + b:w0 + nb * j + b + 1] for j in range(4)]
                if bias is None:
                    step(ts(dst, src[:, b, 0:S], taps[0], None, ALU.mult))
                else:
                    step(ts(dst, src[:, b, 0:S], taps[0], bias, ALU.mult, ALU.add))
                for j in range(1, 4):
                    ins = stt(dst, src[:, b, j:j + S], taps[j], dst, ALU.mult, ALU.add)
                    step(ins)

            for n in range(6):
                moved(dve, f"gq{n}")
                for b in (2 * n, 2 * n + 1):
                    conv(GCO[:, b, :], GIN, V_GCW, 12, b)
                if n % 2:
                    dve.sem_inc(E("gconv"), 1)
            for n in range(3):
                dve.wait_ge(E("gsig"), n + 1)
                step(tt(GCO[:, 4 * n:4 * n + 4, :], GCO[:, 4 * n:4 * n + 4, :], GSIG[:, 4 * n:4 * n + 4, :],
                        ALU.mult))
                dve.sem_inc(E("gsilu_qk" if n < 2 else "gsilu_v"), 1)
            dve.sem_inc(E("gsilu"), 1)
            dve.wait_ge(E("qb_zero"), 4)
            [moved(dve, f"ss{n}") for n in range(4)]
            step(nc_v.reciprocal(RN, RN))
            step(tt(KT, GCO[:, 4:8, :], RN[:, 4:8, :], ALU.mult))
            dve.sem_inc(E("khat"), 1)
            for a in range(2):
                h = slice(64 * a, 64 * a + 64)
                step(stt(QB[h, :, a, :], GCO[h, 0:4, :], GK ** -0.5, RN[h, 0:4, :], ALU.mult, ALU.mult))
            dve.sem_inc(E("rn_done"), 1)
            for n in range(2):
                full(dve, f"bb{n}")
                for a in range(2):
                    h = slice(64 * a, 64 * a + 64)
                    ins = tt(KB[h, 2 * n:2 * n + 2, a, :], ps(f"bb{n}")[h].rearrange("p (c s) -> p c s", s=S),
                             KT[h, 2 * n:2 * n + 2, :], ALU.mult)
                ins.then_inc(free(f"bb{n}"), 1)
                dve.wait_ge(free(f"bb{n}"), uses[f"bb{n}"][1])
            dve.sem_inc(E("kb_ready"), 1)
            [moved(dve, f"gb{n}") for n in range(2)]
            for a in range(2):
                h = slice(64 * a, 64 * a + 64)
                step(tt(QG[h], QB[h, :, a, :], EG[h], ALU.mult))
            dve.wait_ge(E("egc"), 1)
            moved(dve, "rc")
            egc = TS[:, 8:24].rearrange("p (t h) -> p t h", t=NT)
            step(tt(BG, egc, RC[:, :, 0, 96:104], ALU.mult))
            for t in range(NT):
                full(dve, f"vt{t}")
                tt(BV[:, t, :].rearrange("p (h e) -> p h e", h=GH), ps(f"vt{t}").rearrange("p (h e) -> p h e", h=GH),
                   RC[:, t, 0, 96:104].unsqueeze(2).to_broadcast([P, GH, GK]), ALU.mult).then_inc(free(f"vt{t}"), 1)
            for t in range(NT):
                full(dve, f"kt{t}")
                k3 = ps(f"kt{t}").rearrange("p (h e) -> p h e", h=GH)
                tt(KBE[:, t, :].rearrange("p (h e) -> p h e", h=GH), k3,
                   BG[:, t, :].unsqueeze(2).to_broadcast([P, GH, GK]), ALU.mult)
                tt(KDE[:, t, :].rearrange("p (h e) -> p h e", h=GH), k3,
                   RC[:, t, 1, 64:72].unsqueeze(2).to_broadcast([P, GH, GK]), ALU.mult).then_inc(free(f"kt{t}"), 1)
                dve.wait_ge(free(f"kt{t}"), uses[f"kt{t}"][1])
            for t in range(NT):
                for h in range(GH):
                    if t == 0 and h % 2 == 0:
                        full(dve, f"gr{h // 2}")
                    ins = stt(GAM[:, 2 * t + h // 4, (h % 4) * P:(h % 4 + 1) * P],
                              ps(f"gr{h // 2}")[:, (h % 2) * S + t * P:(h % 2) * S + (t + 1) * P],
                              RC[:, t, 0, 64 + h:65 + h], CM[:, K_GTRI], ALU.subtract, ALU.add)
                    if t == 1 and h % 2 == 1:
                        ins.then_inc(free(f"gr{h // 2}"), 1)
                    if t == 0 and h % 4 == 3:
                        ins.then_inc(E("gam_arg"), 1)
            for n in range(4):
                dve.wait_ge(free(f"gr{n}"), uses[f"gr{n}"][1])
            dve.sem_inc(E("gam_arg"), 2)
            plane4 = lambda k: CM[:, k].unsqueeze(1).to_broadcast([P, 4, P])
            quad = lambda ap: ap.rearrange("p (q n) -> p q n", q=4)
            for n in range(4):
                full(dve, f"at{n}")
                dve.wait_ge(E("gam"), n + 1)
                tt(AT[:, n, :], ps(f"at{n}"), GAM[:, n, :], ALU.mult).then_inc(free(f"at{n}"), 1)
                dve.wait_ge(free(f"at{n}"), uses[f"at{n}"][1])
                step(tt(quad(XTi[:, n, :]), quad(AT[:, n, :]), plane4(K_L0T), ALU.mult))
                step(tt(quad(XTi[:, n, :]), plane4(K_ID), quad(XTi[:, n, :]), ALU.subtract))
                dve.sem_inc(E("xt1"), 1)
            for n in range(4):
                full(dve, f"pt{n}")
                tt(PT[:, n, :], ps(f"pt{n}"), GAM[:, n, :], ALU.mult).then_inc(free(f"pt{n}"), 1)
            for k in range(1, 6):
                for n in range(4):
                    full(dve, f"y{k}{n}")
                    tt(quad(Y_[:, n, :]), quad(ps(f"y{k}{n}")), plane4(K_L0T + k), ALU.mult).then_inc(free(f"y{k}{n}"), 1)
                if k < 5:
                    for n in range(4):
                        full(dve, f"z{k}{n}")
                        tt(X_[:, n, :], X_[:, n, :], ps(f"z{k}{n}"), ALU.subtract).then_inc(free(f"z{k}{n}"), 1)
                for n in range(4):
                    full(dve, f"t{k}{n}")
                    tt(XTi[:, n, :], XTi[:, n, :], ps(f"t{k}{n}"), ALU.subtract).then_inc(free(f"t{k}{n}"), 1)
                if k == 1:
                    for n in range(4):
                        moved(dve, f"lx{n}")
                        for b in (2 * n, 2 * n + 1):
                            conv(XA[:, b, :], LX, V_CW, 8, b, VC[:, V_CB + b:V_CB + b + 1])
                    dve.sem_inc(E("xa_ready"), 1)
                    dve.sem_inc(E("lx_free"), 1)
            dve.wait_ge(free("pt3"), uses["pt3"][1])
            
            dve.sem_inc(E("xt_free"), 1)
            nc_v.memset(ST, 0.0).then_inc(E("state"), 1)
            [moved(dve, f"u{t}") for t in range(NT)]
            for c in range(NC):
                t, a = c // 2, 64 * (c % 2)
                h = slice(a, a + 64)
                full(dve, f"ws{c}")
                tt(DE[h, t, :], U_[h, t, :], ps(f"ws{c}")[h], ALU.subtract).then_inc(free(f"ws{c}"), 1)
                if c == 0:
                    dve.wait_ge(E("state"), 1)
                full(dve, f"sn{c}")
                tt(quad(STT), quad(ps(f"sn{c}")), plane4(K_BLK), ALU.mult).then_inc(free(f"sn{c}"), 1)
                dve.wait_ge(free(f"sn{c}"), uses[f"sn{c}"][1])
                if c < NC - 1:
                    for j in range(GP):
                        ins = stt(ST[:, j * P:(j + 1) * P], ST[:, j * P:(j + 1) * P],
                                  EG[:, j, c * CH + CH - 1:c * CH + CH], STT[:, j * P:(j + 1) * P],
                                  ALU.mult, ALU.add)
                    ins.then_inc(E("state"), 1)
                    dve.wait_ge(E("state"), c + 2)
            for t in range(NT):
                full(dve, f"o{t}")
                nc_v.tensor_copy(OS[:, t, :], ps(f"o{t}")).then_inc(free(f"o{t}"), 1)
                dve.wait_ge(free(f"o{t}"), uses[f"o{t}"][1])
                step(tt(OQ[:, t, :], OS[:, t, :], OS[:, t, :], ALU.mult))
                nc_v.reduce_sum(TS[:, 8 * t:8 * t + 8], OQ[:, t, :].rearrange("p (h e) -> p h e", h=GH),
                                AX.X).then_inc(E("oss"), 1)
                dve.wait_ge(E("osq"), t + 1)
                step(nc_v.reciprocal(TS[:, 8 * t:8 * t + 8], TS[:, 8 * t:8 * t + 8]))
                step(tt(OQ[:, t, :].rearrange("p (h e) -> p h e", h=GH), OS[:, t, :].rearrange("p (h e) -> p h e", h=GH),
                        TS[:, 8 * t:8 * t + 8].unsqueeze(2).to_broadcast([P, GH, GK]), ALU.mult))
                dve.sem_inc(E("o_norm"), 1)
            dve.wait_ge(E("zsig"), 1)
            step(tt(GZ, GZ, LT[:, 0:4, :], ALU.mult))
            step(ts(GZ, GZ, VC[:, V_GG:V_GG + 1], None, ALU.mult))
            for t in range(NT):
                full(dve, f"ot{t}")
                tt(HC[:, :, t * P:(t + 1) * P], ps(f"ot{t}").rearrange("p (j s) -> p j s", j=GP),
                   GZ[:, :, t * P:(t + 1) * P], ALU.mult).then_inc(free(f"ot{t}"), 1)
                dve.wait_ge(free(f"ot{t}"), uses[f"ot{t}"][1])
            dve.sem_inc(E("hc_ready"), 1)
            for n in range(2):
                full(dve, f"mr{n}")
                for m in range(2):
                    h = 2 * n + m
                    row = ps(f"mr{n}")[:, m * S:(m + 1) * S]
                    stt(ME[:, h, 0, :], row[:, 0:P], RC[:, 0, 0, h:h + 1], CM[:, K_MTRI], ALU.add, ALU.add)
                    ts(ME[:, h, 1, :], row[:, P:2 * P], RC[:, 0, 0, h:h + 1], None, ALU.add)
                    ins = stt(ME[:, h, 2, :], row[:, P:2 * P], RC[:, 1, 0, h:h + 1], CM[:, K_MTRI], ALU.add,
                              ALU.add)
                ins.then_inc(free(f"mr{n}"), 1)
                dve.wait_ge(free(f"mr{n}"), uses[f"mr{n}"][1])
                dve.sem_inc(E("me_arg"), 1)
            dve.wait_ge(E("me"), 2)
            for j in range(2):
                full(dve, f"ms{j}0")
                tt(MS[:, 2 * j:2 * j + 2, 0:2, :], ps(f"ms{j}0").rearrange("p (a b n) -> p a b n", a=2, b=2),
                   ME[:, 2 * j:2 * j + 2, 0:2, :], ALU.mult).then_inc(free(f"ms{j}0"), 1)
            for j in range(2):
                full(dve, f"ms{j}1")
                tt(MS[:, 2 * j:2 * j + 2, 2, :], ps(f"ms{j}1")[:, 0:256].rearrange("p (a n) -> p a n", a=2),
                   ME[:, 2 * j:2 * j + 2, 2, :], ALU.mult).then_inc(free(f"ms{j}1"), 1)
            for nm in ("ms00", "ms10", "ms01", "ms11"):
                dve.wait_ge(free(nm), uses[nm][1])
            dve.sem_inc(E("ms_ready"), 2)
            for t in range(NT):
                for j in range(2):
                    full(dve, f"mn{t}{j}")
                    o3 = ps(f"mn{t}{j}")[:, 0:258].rearrange("p (a e) -> p a e", a=2)
                    den = RT2[:, 16 + 4 * t + 2 * j:18 + 4 * t + 2 * j]
                    step(nc_v.tensor_copy(den.unsqueeze(2), o3[:, :, 128:129]))
                    step(stt(den, den, -1.0, den, ALU.mult, ALU.max))
                    step(tt(den, den, RC[:, t, 0, 32 + 2 * j:34 + 2 * j], ALU.max))
                    step(nc_v.reciprocal(den, den))
                    for a in range(2):
                        ins = ts(MN[:, t, 2 * j + a, :], o3[:, a, 0:128], den[:, a:a + 1], None, ALU.mult)
                    ins.then_inc(free(f"mn{t}{j}"), 1)
                    dve.wait_ge(free(f"mn{t}{j}"), uses[f"mn{t}{j}"][1])
                dve.sem_inc(E("mn_scaled"), 1)
            for t in range(NT):
                dve.wait_ge(E("mss"), 2 * t + 2)
                step(nc_v.reciprocal(RT2[:, 8 + 4 * t:12 + 4 * t], RT2[:, 8 + 4 * t:12 + 4 * t]))
                for h in range(MH):
                    ins = ts(MQ2[:, t, h, :], MN[:, t, h, :], RT2[:, 8 + 4 * t + h:9 + 4 * t + h], None, ALU.mult)
                ins.then_inc(E("mn_norm"), 1)
            for h in range(MH):
                ins = ts(MO[:, h, :], MO[:, h, :], VC[:, V_MG + h:V_MG + h + 1], None, ALU.mult)
            step(ins)
            for t in range(NT):
                full(dve, f"mt{t}")
                tt(HB[:, :, t * P:(t + 1) * P], ps(f"mt{t}").rearrange("p (h s) -> p h s", h=MH),
                   MO[:, :, t * P:(t + 1) * P], ALU.mult).then_inc(free(f"mt{t}"), 1)
                dve.wait_ge(free(f"mt{t}"), uses[f"mt{t}"][1])
            dve.sem_inc(E("hb_ready"), 1)
            dve.wait_ge(E("lgates"), 1)
            dve.wait_ge(E("la"), 1)
            [moved(dve, f"ly{n}") for n in range(4)]
            step(tt(LR, LY, LY, ALU.mult))
            step(ts(LR, LR, 0.044715, 1.0, ALU.mult, ALU.add))
            step(tt(LR, LR, LY, ALU.mult))
            dve.sem_inc(E("gelu_arg"), 1)
            step(ts(LT, LU, 1.0, None, ALU.add))
            step(nc_v.reciprocal(LT, LT))
            step(tt(LU, LU, LT, ALU.mult))
            dve.sem_inc(E("lu_arg"), 1)
            step(tt(LG, LG, XA, ALU.mult))
            dve.wait_ge(E("gelu_tanh"), 1)
            step(stt(LY, LR, 1.0, LY, ALU.add, ALU.mult))
            dve.wait_ge(E("lu"), 1)
            step(tt(LU, LU, LG, ALU.mult))
            for b in range(NB):
                ins = nc_v.tensor_tensor_scan(LT[:, b, :], LA[:, b, :], LU[:, b, :], 0.0, ALU.mult, ALU.add)
            step(ins)
            step(stt(LY, LT, 0.5, LY, ALU.mult, ALU.mult))
            dve.sem_inc(E("ha_ready"), 1)
            for n in range(3):
                for d in range(4):
                    k = 4 * n + d
                    full(dve, f"br{n}{d}")
                    moved(dve, f"ga{n}{d}")
                    m2 = MG[:, 2 * d:2 * d + 2, :].rearrange("p c s -> p (c s)")
                    dst = m2 if n == 0 else MT[k % 2]
                    tt(dst, ps(f"br{n}{d}"), SG[k % 2], ALU.mult).then_inc(free(f"br{n}{d}"), 1)
                    dve.wait_ge(free(f"br{n}{d}"), uses[f"br{n}{d}"][1])
                    if n:
                        step(tt(m2, m2, MT[k % 2], ALU.add))
            dve.sem_inc(E("merged"), 1)
            for d in range(4):
                full(dve, f"wo{d}")
                stt(X1[:, :, d * GW:(d + 1) * GW], XTOK[:, :, d * GW:(d + 1) * GW], ALPHA,
                    ps(f"wo{d}").rearrange("p (t n) -> p t n", t=NT), ALU.mult, ALU.add).then_inc(free(f"wo{d}"), 1)
            for d in range(4):
                dve.wait_ge(free(f"wo{d}"), uses[f"wo{d}"][1])
            if stop:
                dve.sem_inc(E("stop"), 1)
                return
            dve.sem_inc(E("mix_done"), 1)
            dve.sem_inc(E("mix_done_pe"), 1)

            def layer_norm(v, var_event, sd_event, in_event, n):
                bn = RT2[:, 0:24].rearrange("p (t k) -> p t k", t=NT)
                for t in range(NT):
                    for h in range(2):
                        ins = nc_v.bn_stats(bn[:, t, 6 * h:6 * h + 6], v[:, t, h * 512:(h + 1) * 512])
                step(ins)
                for t in range(NT):
                    ins = nc_v.bn_aggr(RT2[:, 24 + 2 * t:26 + 2 * t], bn[:, t, :])
                step(ins)
                nc_v.tensor_copy(TS[:, 8:10], RT2[:, 25:28:2]).then_inc(E(var_event), 1)
                dve.wait_ge(E(sd_event), 1)
                step(nc_v.reciprocal(TS[:, 8:10], TS[:, 8:10]))
                for t in range(NT):
                    ins = ts(v[:, t, :], v[:, t, :], RT2[:, 24 + 2 * t:25 + 2 * t], TS[:, 8 + t:9 + t],
                             ALU.subtract, ALU.mult)
                step(ins)
                dve.wait_ge(E(in_event), 32)
                step(tt(v, v, LNG.unsqueeze(1).to_broadcast([P, NT, D]), ALU.mult))
                step(tt(v, v, LNB.unsqueeze(1).to_broadcast([P, NT, D]), ALU.add))

            layer_norm(X1, "ln1_var", "ln1_sd", "ln1_in", 1)
            dve.sem_inc(E("x1_ready"), 1)
            full(dve, "lgt")
            dve.wait_ge(E("rout_in"), 32)
            step(nc_v.memset(LOG[:, :, NE:], 3e38))
            tt(LOG[:, :, 0:NE], ps("lgt")[:, 0:64].rearrange("p (t e) -> p t e", t=NT), RBIAS.unsqueeze(1).to_broadcast([P, NT, NE]),
               ALU.add).then_inc(free("lgt"), 1)
            dve.wait_ge(free("lgt"), uses["lgt"][1])
            for t in range(NT):
                step(nc_v.max(TOP[:, t, :], LOG[:, t, 0:NE]))
                step(ts(EXL[:, t, :], LOG[:, t, 0:NE], TOP[:, t, 0:1], None, ALU.subtract))
            dve.sem_inc(E("exl_arg"), 1)
            step(nc_v.memset(TOP[:, :, 4:8], 3e38))
            for t in range(NT):
                step(nc_v.match_replace(out=LOGR[:, t, :], in_to_replace=TOP[:, t, :], in_values=LOG[:, t, :],
                                        imm_value=-3e38))
            step(ts(SEL, LOGR[:, :, 0:NE], -2.9e38, None, ALU.is_lt))
            dve.sem_inc(E("sel_ready"), 1)
            step(nc_v.memset(POS, -1.0))
            step(nc_v.memset(GAT, 0.0))
            dve.wait_ge(E("exl"), 1)
            step(tt(EXL, EXL, SEL, ALU.mult))
            step(nc_v.reduce_sum(RT2[:, 0:2], EXL, AX.X))
            step(nc_v.reciprocal(RT2[:, 0:2], RT2[:, 0:2]))
            step(tt(GAT[:, :, 0:NE], EXL, RT2[:, 0:2].unsqueeze(2).to_broadcast([P, NT, NE]), ALU.mult))
            dve.sem_inc(E("gates_ready"), 1)
            for r in range(1, ROUNDS):
                ins = nc_v.tensor_copy(GAT[:, :, r * NE:(r + 1) * NE], GAT[:, :, 0:NE])
            step(ins)
            full(dve, "cnt")
            c3 = ps("cnt")[:, 0:64].rearrange("p (t e) -> p t e", t=NT)
            step(stt(POS[:, :, 0:NE], c3, 1.0, SEL, ALU.add, ALU.mult))
            step(nc_v.tensor_reduce(RT2[:, 4:5], ps("cnt")[:, 64:96], AX.X, ALU.max))
            dve.sem_inc(free("cnt"), 1)
            for r in range(ROUNDS - 1, -1, -1):
                ins = ts(POS[:, :, r * NE:(r + 1) * NE], POS[:, :, 0:NE], 1.0 + r * CAP, None, ALU.subtract)
                step(ins)
            step(ts(RT2[:, 5:6], RT2[:, 4:5], float(CAP), 1.0, ALU.is_gt, ALU.add))
            for r in range(2, ROUNDS):
                step(stt(RT2[:, 5:6], RT2[:, 4:5], float(r * CAP), RT2[:, 5:6], ALU.is_gt, ALU.add))
            nc_v.tensor_copy(NR[:, :], RT2[:, 5:6]).then_inc(E("rounds_ready"), 1)
            dve.wait_ge(E("rounds_ready"), 1)
            nc_v.memset(YS, 0.0)
            nc_v.memset(GTS, 0.0).then_inc(E("ys_ready"), 1)

            def onehot(i):
                for t in range(NT):
                    ins = ts(ONE[:, t, :], CM[:, K_IOTA, 0:CAP], POS[:, t, bass.ds(i, 1)], None, ALU.is_equal)
                ins.then_inc(E("onehot"), 1)

            def gated(i):
                for t in range(NT):
                    ins = ts(GAD[:, t, :], CM[:, K_IOTA], POS[:, t, bass.ds(i, 1)],
                             GAT[:, t, bass.ds(i, 1)], ALU.is_equal, ALU.mult)
                ins.then_inc(E("gated"), 1)

            def pick(e):
                nc_v.tensor_copy(PICK[0:NE, :], CM[0:NE, K_ID, bass.ds(e, 1)].to_broadcast([NE, CAP])
                                 ).then_inc(E("pick"), 1)
            onehot(0)
            rounds = dve.value_load(NR[0:1, 0:1], min_val=1, max_val=ROUNDS)
            with dve.Fori(0, rounds) as r, dve.Fori(0, NE) as e:
                i = r * NE + e
                pick(e)
                gated(i)
                dve.wait_ge(E("xg_full"), i + 1)
                onehot(i + 1)
                dve.wait_ge(E("w1_used"), KD * i + KD)
                ts(GLU, PS[:, 0, :], LIMIT, None, ALU.min).then_inc(E("glu_ready"), 1)
                ts(LIN, PS[:, 1, :], -LIMIT, LIMIT, ALU.max, ALU.min).then_inc(E("lin_clipped"), 1)
                dve.wait_ge(E("glu_ready"), i + 1)
                dve.wait_ge(E("lin_clipped"), i + 1)
                stt(LIN, LIN, 1.0, GLU, ALU.add, ALU.mult).then_inc(E("lin_glu"), 1)
                dve.wait_ge(E("lin_glu"), i + 1)
                dve.wait_ge(E("sig_ready"), i + 1)
                tt(HID, LIN, SIG, ALU.mult).then_inc(E("hid_ready"), 1)
                dve.wait_ge(E("ht_full"), i + 1)
                nc_v.tensor_copy(HT, PS[:, 3, :].rearrange("p (q n) -> p q n", q=4)).then_inc(E("ht_ready"), 1)
            dve.wait_ge(E("acc_done"), 1)
            for t in range(NT):
                ins = stt(X1[:, t, :], X1[:, t, :], ALPHA, PS[:, 4 + 2 * t:6 + 2 * t, :]
                          .rearrange("p a b -> p (a b)"), ALU.mult, ALU.add)
            ins.then_inc(E("x2"), 1)
            dve.wait_ge(E("x2"), 1)
            layer_norm(X1, "ln2_var", "ln2_sd", "ln2_in", 2)
            dve.sem_inc(E("out_ready"), 1)


NAMES = ["x", "w_in", "lru_conv_w", "lru_conv_b", "lru_wa", "lru_ba", "lru_wx", "lru_bx", "lru_lambda",
         "ml_i_bias", "ml_f_bias", "ml_norm_g", "gd_conv_w", "gd_a_log", "gd_dt_bias", "gd_norm_g",
         "w_br_lru", "w_br_ml", "w_br_gd", "w_out", "ln1_g", "ln1_b", "router_w", "router_b",
         "exp_w1", "exp_b1", "exp_w2", "exp_b2", "ln2_g", "ln2_b"]


def kernel(**inputs):
    import concourse.bacc as bacc
    from concourse.bass_utils import run_bass_kernel_spmd

    nc = bacc.Bacc("TRN2", target_bir_lowering=False, num_devices=1)
    arrays, args = {}, []
    for name in NAMES + ["planes"]:
        a = constant_planes() if name == "planes" else np.ascontiguousarray(inputs[name])
        arrays[name] = a
        args.append(nc.dram_tensor(name, a.shape, mybir.dt.from_np(a.dtype), kind="ExternalInput").ap())
    out = nc.dram_tensor("out", (1, S, D), F32, kind="ExternalOutput").ap()
    layer_kernel(nc, False, {}, *args, out)
    result = run_bass_kernel_spmd(nc, [arrays], core_ids=[0])
    return result.results[0]["out"]
```

```python
from contextlib import ExitStack

import numpy as np

import concourse.bass as bass
from concourse import mybir

F32 = mybir.dt.float32
I32 = mybir.dt.int32
ALU = mybir.AluOpType
ACT = mybir.ActivationFunctionType
AX = mybir.AxisListType

P = 128
S = 256
NT = S // P
D = 1024
KD = D // P
LW = 1024
NB = LW // P
MH, MQ, MV = 4, 64, 128
GH, GK = 8, 64
GP = GH // 2
CH = 64
NC = S // CH
NE, TOPK, FF = 32, 4, 1024
KF = FF // P
EC = KD + KF // 2
SLOTS = 16
EB = 4
CAP = 64
ROUNDS = S // CAP
LRU_C = 8.0
ALPHA = 2.0 ** 0.25
LN_EPS, RMS_EPS = 1e-5, 1e-6
LIMIT, SWIGLU = 7.0, 1.702
NEG = -1e30

C_LX, C_LY = 0, LW
C_MQ = 2 * LW
C_MK = C_MQ + MH * MQ
C_MV = C_MK + MH * MQ
C_MI = C_MV + MH * MV
C_MO = C_MI + 2 * MH
C_GQ = C_MO + MH * MV
C_GK = C_GQ + GH * GK
C_GV = C_GK + GH * GK
C_GA = C_GV + GH * GK
C_GZ = C_GA + 2 * GH
C_GT = C_GZ + GH * GK

GW = 256
WBUFS = 3

(K_ID, K_BLK, K_L0T, K_L1, K_L2, K_L3, K_L4, K_L5, K_MTRI, K_GTRI, K_BEFORE, K_ONES, K_IOTA,
 K_COLS, K_RST0, K_RST1) = range(16)
NPLANES = 16

V_CW, V_CB, V_BA, V_BX, V_LAM, V_GCW, V_MG, V_GG = 0, 32, 40, 48, 56, 64, 112, 116


def constant_planes():
    c = np.zeros((P, NPLANES, P), np.float32)
    r, q = np.arange(P)[:, None], np.arange(P)[None, :]
    c[:, K_ID] = r == q
    c[:, K_BLK] = r // CH == q // CH
    c[:, K_L0T] = (q % 2 == 1) & (r == q - 1)
    for k in range(1, 6):
        b = 2 ** k
        c[:, K_L0T + k] = ((r // b) % 2 == 1) & (q // b == r // b - 1)
    c[:, K_MTRI] = np.where(r <= q, 0.0, NEG)
    c[:, K_GTRI] = np.where((r <= q) & (r // CH == q // CH), 0.0, NEG)
    c[:, K_BEFORE] = r < q
    c[:, K_ONES] = 1.0
    c[:, K_IOTA] = q % CAP + 0 * r
    c[:, K_COLS, 0:1] = np.where((r >= 32) & (r < 64), -1.0, 1.0)
    c[:, K_COLS, 1:2] = np.where((r >= 32) & (r < 96), -1.0, 0.0)
    reset = np.ones((P, S), np.float32)
    reset[64:96, ::CH] = 0.0
    c[:, K_RST0:K_RST1 + 1] = reset.reshape(P, 2, P)
    return c.reshape(P, NPLANES * P)


def branch_items():
    order = [(kind, n, d) for n in range(2) for d in range(4) for kind in ("ga", "br")]
    return order + [("ga", 2, 0), ("ga", 2, 1), ("br", 2, 0), ("ga", 2, 2), ("br", 2, 1), ("ga", 2, 3),
                    ("br", 2, 2), ("br", 2, 3)]


FILL = (("mq",), ("mk", "mr0", "mr1"), ("lg",), ("ms00", "ms10", "ms01", "ms11", "mv0"), ("mv1",),
        ("mn", "mo0"), ("mo1",), ("mt", "gz0"), ("gz1",), ("ga00",))


def weight_stream():
    seq = [(f"gq{n}", "w_in", C_GQ + GW * n) for n in range(6)]
    seq += [(f"lx{n}", "w_in", C_LX + GW * n) for n in range(4)]
    seq += [(f"ly{n}", "w_in", C_LY + GW * n) for n in range(4)]
    seq += [("mq", "w_in", C_MQ), ("mk", "w_in", C_MK), ("lg7", "lru", 0)]
    seq += [(f"mv{n}", "w_in", C_MV + GW * n) for n in range(2)]
    seq += [(f"mo{n}", "w_in", C_MO + GW * n) for n in range(2)]
    seq += [(f"gz{n}", "w_in", C_GZ + GW * n) for n in range(2)]
    for kind, n, d in branch_items():
        if kind == "ga":
            seq += [(f"ga{n}{d}", "w_in", C_GT + D * n + GW * d)]
        else:
            seq += [(f"br{n}{d}", ("w_br_lru", "w_br_ml", "w_br_gd")[n], GW * d)]
    seq += [(f"wo{d}", "w_out", GW * d) for d in range(4)]
    return seq


def bank_uses():
    order = [(f"xT{t}{h}", 2 * t + h) for t in range(NT) for h in range(2)]
    proj = 0

    def p(*names):
        nonlocal proj
        for name in names:
            order.append((name, proj % 4))
            proj += 1
    p("gq0")
    order += [("vec", 4), ("small", 5)]
    p(*[f"gq{n}" for n in range(1, 6)], "lx0", "lx1")
    order += [("rc", 6)]
    order += [("ss2", 4), ("ss3", 5), ("ss0", 6), ("ss1", 7)]
    p("lx2", "lx3")
    order += [("bb0", 4), ("bb1", 5), ("gb0", 6), ("gb1", 7)]
    p("ly0")
    order += [("vt0", 4), ("vt1", 5), ("kt0", 6), ("kt1", 7)]
    order += [(f"gr{n}", 4 + n) for n in range(4)]
    p("ly1")
    order += [(f"at{n}", 4 + n) for n in range(4)]
    p("ly2")
    order += [(f"pt{n}", 4 + n) for n in range(4)]
    p("ly3")
    order += [(f"x1{n}", 4 + n) for n in range(4)]
    parts = {"lg": [f"lg{b}" for b in range(NB)], "mn": ["mn00", "mn01", "mn10", "mn11"],
             "mt": ["mt0", "mt1"]}

    def fill(slot):
        for name in FILL[slot]:
            p(*parts.get(name, [name]))
    for k in range(1, 6):
        order += [(f"y{k}{n}", 4 + n) for n in range(4)]
        fill(2 * k - 2)
        if k < 5:
            order += [(f"z{k}{n}", 4 + n) for n in range(4)]
        order += [(f"t{k}{n}", 4 + n) for n in range(4)]
        fill(2 * k - 1)
    order += [("u0", 4), ("u1", 5), ("w0", 6), ("w1", 7)]
    items = [f"{kind}{n}{d}" for kind, n, d in branch_items()][1:]
    p(items.pop(0))
    for c in range(NC):
        order += [(f"ws{c}", 4)]
        p(items.pop(0))
        if c % 2 == 0:
            order += [(f"o{c // 2}", 5 + c // 2)]
        if c < NC - 1:
            order += [(f"sn{c}", 7)]
        p(items.pop(0))
    p(items.pop(0), items.pop(0))
    order += [("ot0", 4)]
    p(items.pop(0), items.pop(0))
    order += [("ot1", 7)]
    p(*items)
    order += [("wo00", 0), ("wo01", 1), ("wo10", 2), ("x1T00", 4), ("x1T01", 5), ("wo11", 3)]
    order += [("lgt0", 0), ("x1T10", 1), ("x1T11", 2), ("lgt1", 3), ("cnt", 0), ("gT", 3)]
    count = [0] * 8
    uses = {}
    for name, bank in order:
        count[bank] += 1
        assert name not in uses, name
        uses[name] = (bank, count[bank])
    return uses, count


def layer_kernel(nc, x, w_in, lru_conv_w, lru_conv_b, lru_wa, lru_ba, lru_wx, lru_bx,
                 lru_lambda, ml_i_bias, ml_f_bias, ml_norm_g, gd_conv_w, gd_a_log, gd_dt_bias,
                 gd_norm_g, w_br_lru, w_br_ml, w_br_gd, w_out, ln1_g, ln1_b, router_w, router_b,
                 exp_w1, exp_b1, exp_w2, exp_b2, ln2_g, ln2_b, planes, out):
    uses, bank_total = bank_uses()
    stream = weight_stream()
    stream_at = {name: n for n, (name, _, _) in enumerate(stream)}

    def stream_value(n):
        return 16 * sum(2 if src == "lru" else 1 for _, src, _ in stream[n % WBUFS:n + 1:WBUFS])

    sources = {"w_in": w_in, "w_br_lru": w_br_lru, "w_br_ml": w_br_ml, "w_br_gd": w_br_gd,
               "w_out": w_out}
    with ExitStack() as ctx:
        sems = {}

        def E(name):
            if name not in sems:
                sems[name] = ctx.enter_context(nc.semaphore("s_" + name))
            return sems[name]

        RING = ctx.enter_context(nc.sbuf_tensor("ring", [P, 96 * 256], F32))
        MIX = ctx.enter_context(nc.sbuf_tensor("mix", [P, 28400], F32))
        NR = ctx.enter_context(nc.sbuf_tensor("rounds", [P, 1], I32))
        PS = ctx.enter_context(nc.psum_tensor("ps", [P, 8, 512], F32))

        def area(base, kb, words):
            return base[:, int(kb * 256):int(kb * 256) + words]

        WB = [area(MIX, 8 * n, 2048).rearrange("p (c n) -> p c n", n=GW) for n in range(WBUFS)]
        XTOK = area(MIX, 24, 2048).rearrange("p (t d) -> p t d", t=NT)
        XT = area(MIX, 32, 2048).rearrange("p (c s) -> p c s", s=S)
        LX = area(MIX, 40, NB * 259).rearrange("p (b s) -> p b s", s=259)
        LY = area(MIX, 48.25, 2048).rearrange("p (b s) -> p b s", s=S)
        XA = area(MIX, 56.25, 2048).rearrange("p (b s) -> p b s", s=S)
        GZ = area(MIX, 64.25, 1024).rearrange("p (j s) -> p j s", s=S)
        MO = area(MIX, 68.25, 1024).rearrange("p (j s) -> p j s", s=S)
        V1 = area(MIX, 72.25, NT * MH * 129).rearrange("p (t h e) -> p t h e", t=NT, h=MH)
        QM = area(MIX, 76.5, 1024).rearrange("p (j a s) -> p j a s", j=2, a=2)
        MK = area(MIX, 80.5, 512).rearrange("p (j s) -> p j s", s=S)
        HB = area(MIX, 82.5, 1024).rearrange("p (j s) -> p j s", s=S)
        HC = area(MIX, 86.5, 1024).rearrange("p (j s) -> p j s", s=S)
        CM = area(MIX, 90.5, NPLANES * P).rearrange("p (k n) -> p k n", n=P)
        VR = area(MIX, 98.5, P)
        VC = area(MIX, 99, P)
        RB = area(MIX, 99.5, S)
        RW = area(MIX, 100.5, S)
        RX = area(MIX, 101.5, S)
        NM = area(MIX, 102.5, S)
        ROUT = area(MIX, 103.5, 256).rearrange("p (c e) -> p c e", e=NE)
        RC = area(MIX, 104.5, 512).rearrange("p (t k n) -> p t k n", t=2, k=2)
        SC = area(MIX, 110.5, 110)
        RBIAS = SC[:, 0:32]
        BIAS, ALOG, COEF = SC[:, 32:33], SC[:, 33:34], SC[:, 34:35]
        LSP = SC[:, 40:48]
        NLSP = SC[:, 48:56]
        BG = SC[:, 56:72].rearrange("p (t h) -> p t h", t=NT)
        TS = SC[:, 72:104]
        ident = CM[:, K_ID]

        GIN = area(RING, 0, 12 * 259).rearrange("p (b s) -> p b s", s=259)
        X_ = area(RING, 0, 2048).rearrange("p (n q) -> p n q", q=512)
        XTi = area(RING, 8, 2048).rearrange("p (n q) -> p n q", q=512)
        AT = area(RING, 16, 2048).rearrange("p (n q) -> p n q", q=512)
        Y_ = area(RING, 24, 2048).rearrange("p (n q) -> p n q", q=512)
        GCO = area(RING, 16, 12 * S).rearrange("p (b s) -> p b s", s=S)
        GSIG = area(RING, 48, 12 * S).rearrange("p (b s) -> p b s", s=S)
        GAM = area(RING, 32, 2048).rearrange("p (n q) -> p n q", q=512)
        PT = area(RING, 40, 2048).rearrange("p (n q) -> p n q", q=512)
        ROWT = [area(RING, 32 + n, S) for n in range(8)]
        QB = area(RING, 48, 2048).rearrange("p (j a s) -> p j a s", j=GP, a=2)
        KB = area(RING, 56, 2048).rearrange("p (j a s) -> p j a s", j=GP, a=2)
        QG = area(RING, 64, 1024).rearrange("p (j s) -> p j s", s=S)
        KT = area(RING, 68, 1024).rearrange("p (j s) -> p j s", s=S)
        KBE = area(RING, 72, 1024).rearrange("p (t n) -> p t n", t=NT)
        KDE = area(RING, 76, 1024).rearrange("p (t n) -> p t n", t=NT)
        BV = area(RING, 80, 1024).rearrange("p (t n) -> p t n", t=NT)
        EG = area(RING, 84, 1024).rearrange("p (j s) -> p j s", s=S)
        RN = area(RING, 88, 2048).rearrange("p (b s) -> p b s", s=S)
        WSM = area(RING, 88, 1024).rearrange("p (c n) -> p c n", n=P)
        SQ = area(RING, 40, 2048).rearrange("p (b s) -> p b s", s=S)
        U_ = area(RING, 48, 1024).rearrange("p (t n) -> p t n", t=NT)
        WT = area(RING, 52, 1024).rearrange("p (t j n) -> p t j n", t=NT, j=GP)
        DE = area(RING, 56, 1024).rearrange("p (t n) -> p t n", t=NT)
        ST = area(RING, 60, 512)
        STT = area(RING, 62, 512)
        OS = area(RING, 24, 1024).rearrange("p (t n) -> p t n", t=NT)
        OQ = area(RING, 28, 1024).rearrange("p (t n) -> p t n", t=NT)
        LR = area(MIX, 40, 2048).rearrange("p (b s) -> p b s", s=S)
        LG = area(RING, 32, 2048).rearrange("p (b s) -> p b s", s=S)
        LU = area(RING, 88, 2048).rearrange("p (b s) -> p b s", s=S)
        ME = area(MIX, 82.5, 1536).rearrange("p (h b n) -> p h b n", h=MH, b=3)
        MN = area(RING, 68, 1024).rearrange("p (t h n) -> p t h n", t=NT, h=MH)
        MSQ = area(MIX, 106.5, 1024).rearrange("p (t h n) -> p t h n", t=NT, h=MH)
        MG = area(MIX, 56.25, 2048).rearrange("p (c s) -> p c s", s=S)
        SG = [area(MIX, 40 + 2 * n, 512) for n in range(4)]
        MT = [area(MIX, 76.5 + 2 * n, 512) for n in range(2)]
        WO3 = area(MIX, 48.25, 2048).rearrange("p (c n) -> p c n", n=GW)
        X1 = area(MIX, 40, 2048).rearrange("p (t d) -> p t d", t=NT)
        LNG = area(MIX, 64.25, 1024)
        LNB = area(MIX, 68.25, 1024)
        X1T = area(MIX, 32, 2048).rearrange("p (c s) -> p c s", s=S)
        B1R = area(MIX, 72.25, 2048)
        SLOT = [area(RING, 8 * n, 2048) for n in range(EC)] + [area(MIX, kb, 2048) for kb in (48.25, 56.25, 24, 32)]
        XG = area(MIX, 0, 512)
        XE = area(MIX, 2, 512).rearrange("p (q n) -> p q n", q=4)
        GLU = area(MIX, 4, 512)
        LIN = area(MIX, 6, 512)
        SIG = area(MIX, 8, 512)
        HID = area(MIX, 10, 512)
        HT = area(MIX, 12, 512).rearrange("p (q n) -> p q n", q=4)
        AID = CM[:, K_MTRI]
        YS = area(MIX, 80.5, 512)
        ONE = area(MIX, 102, NT * CAP).rearrange("p (t n) -> p t n", t=NT)
        GAD = area(MIX, 105.5, NT * P).rearrange("p (t n) -> p t n", t=NT)
        GTS = area(MIX, 104.5, S)
        PICK = area(MIX, 102.5, CAP)
        POS = area(MIX, 99.5, NT * 129).rearrange("p (t n) -> p t n", t=NT)
        GAT = area(MIX, 100.75, NT * 129).rearrange("p (t n) -> p t n", t=NT)
        LOG = area(MIX, 82.5, 80).rearrange("p (t e) -> p t e", t=NT)
        LOGR = area(MIX, 86, 80).rearrange("p (t e) -> p t e", t=NT)
        SEL = area(MIX, 83, 64).rearrange("p (t e) -> p t e", t=NT)
        EXL = area(MIX, 83.25, 64).rearrange("p (t e) -> p t e", t=NT)
        TOP = area(MIX, 83.5, 16).rearrange("p (t e) -> p t e", t=NT)
        RT2 = area(MIX, 98.5, 64)

        def ps(name):
            return PS[:, uses[name][0], :]

        nc_v, nc_s, nc_g = nc.vector, nc.scalar, nc.gpsimd
        block = ctx.enter_context(nc.Block())

        def full(eng, name):
            bank, n = uses[name]
            eng.wait_ge(E(f"bank_full{bank}"), n)

        def moved(eng, name):
            bank, n = uses[name]
            eng.wait_ge(E(f"bank_free{bank}"), n)

        def free(name):
            return E(f"bank_free{uses[name][0]}")

        @block.sync
        def _(sp):
            def load_chunk(n, e):
                c = n % EC
                if c < KD:
                    dst = SLOT[n % SLOTS]
                    src = exp_w1[0, bass.ds(e, 1), c * P:(c + 1) * P, :].rearrange("e p n -> p (e n)")
                else:
                    dst = SLOT[n % SLOTS].rearrange("p (c n) -> p c n", n=D)
                    r = 2 * (c - KD) * P
                    src = exp_w2[0, bass.ds(e, 1), r:r + 2 * P, :].rearrange("e (c p) n -> p (e c) n", p=P)
                sp.dma_start(dst, src).then_inc(E(f"chunk_in{n % SLOTS}"), 16)

            ahead = [stream_at[name] for name in ("br20", "ga22", "br21", "ga23")]
            for t in range(NT):
                sp.dma_start(XTOK[:, t, :], x[0, t * P:(t + 1) * P, :]).then_inc(E(f"x_in{t}"), 16)
            for n, (name, src, col) in enumerate(stream):
                buf, loaded = WB[n % WBUFS], E(f"w_in{n % WBUFS}")
                if name == "wo3":
                    buf, loaded = WO3, E("wo3_in")
                    full(sp, "br03")
                elif n >= WBUFS:
                    full(sp, stream[n - WBUFS][0])
                if src == "lru":
                    both = buf.rearrange("p c n -> p (c n)").rearrange("p (k b n) -> p k b n", k=2, b=NB)
                    sp.dma_start(both[:, 0], lru_wa[0].rearrange("b i j -> i b j")).then_inc(loaded, 16)
                    sp.dma_start(both[:, 1], lru_wx[0].rearrange("b i j -> i b j")).then_inc(loaded, 16)
                    continue
                w = sources[src][0]
                k = w.shape[0] // P
                sp.dma_start(buf[:, 0:k, :], w[:, col:col + GW].rearrange("(c p) n -> p c n", p=P)
                             ).then_inc(loaded, 16)
                if name == "gq1":
                    sp.wait_ge(E("small_zero"), 4)
                    for q, (first, cols) in enumerate(((C_MI, MH), (C_MI + MH, MH), (C_GA, GH), (C_GA + GH, GH))):
                        sp.dma_start(WSM[:, :, 32 * q:32 * q + cols], w_in[0, :, first:first + cols]
                                      .rearrange("(c p) n -> p c n", p=P)).then_inc(E("wsm_in"), 16)
                if n == ahead[0]:
                    for event in ("ha_ready", "hb_ready", "hc_ready"):
                        sp.wait_ge(E(event), 1)
                if n in ahead:
                    load_chunk(ahead.index(n), 0)
            for n in range(len(ahead), EC):
                load_chunk(n, 0)
            full(sp, "wo11")
            load_chunk(EC, 1)
            load_chunk(EC + 1, 1)
            moved(sp, "wo11")
            load_chunk(EC + 2, 1)
            full(sp, "lgt1")
            load_chunk(EC + 3, 1)
            def load_turn(turn, expert, first=0):
                for n in range(first, EB * EC):
                    sp.wait_ge(E("chunk_used"), turn * EB * EC + n - SLOTS + 1)
                    load_chunk(n, expert + n // EC)
            load_turn(0, 0, SLOTS)
            with sp.Fori(1, NE // EB) as q:
                load_turn(q, q * EB)
            sp.wait_ge(E("rounds_ready"), 1)
            rounds = sp.value_load(NR[0:1, 0:1], min_val=1, max_val=ROUNDS)
            with sp.If(rounds > 1):
                with sp.Fori(1, rounds) as r:
                    with sp.Fori(0, NE // EB) as q:
                        load_turn(r * (NE // EB) + q, q * EB)
            for t in range(NT):
                sp.wait_ge(E("out_ready"), t + 1)
                sp.dma_start(out[0, t * P:(t + 1) * P, :], X1[:, t, :]).then_inc(E("stored"), 16)
            sp.wait_ge(E("stored"), 16 * NT)

        @block.gpsimd
        def _(gp):
            cleared = [0]

            def clear(region, value, event):
                cleared[0] += 1
                nc_g.memset(region, value).then_inc(E("cleared"), 1)
                gp.wait_ge(E("cleared"), cleared[0])
                gp.sem_inc(E(event), 1)
            clear(BIAS, 0.0, "small_zero")
            clear(ALOG, 0.0, "small_zero")
            clear(VR, 0.0, "small_zero")
            clear(WSM, 0.0, "small_zero")
            clear(GIN[:, :, 0:3], 0.0, "gin_pad")
            clear(LX[:, :, 0:3], 0.0, "lx_pad")
            clear(RX, 0.0, "rx_zero")
            clear(NM, 0.0, "nm_zero")
            clear(QM[64:128, :, 0, :], 0.0, "qm_zero")
            clear(QM[0:64, :, 1, :], 0.0, "qm_zero")
            clear(V1[:, :, :, 128:129], 1.0, "v1_one")
            gp.wait_ge(E("gsilu"), 1)
            for R in (QB, KB):
                clear(R[64:128, :, 0, :], 0.0, "qb_zero")
                clear(R[0:64, :, 1, :], 0.0, "qb_zero")

        @block.tensor
        def _(pe):
            mm = nc.tensor.matmul

            def take(name):
                bank, n = uses[name]
                if n > 1:
                    pe.wait_ge(E(f"bank_free{bank}"), n - 1)
                return PS[:, bank, :]

            def done(name, ins):
                ins.then_inc(E(f"bank_full{uses[name][0]}"), 1)

            def weights(name):
                n = stream_at[name]
                pe.wait_ge(E(f"w_in{n % WBUFS}"), stream_value(n))
                return WB[n % WBUFS]

            def proj(name, rhs=XT, nk=KD):
                w = weights(name)
                o = take(name)
                for m in range(2):
                    for c in range(nk):
                        ins = mm(o[:, m * S:(m + 1) * S], w[:, c, m * P:(m + 1) * P], rhs[:, c, :],
                                 start=(m == 0 and c == 0), stop=(c == nk - 1), skip_group_check=True)
                done(name, ins)

            def proj_tok(name, lhs, nk=KD):
                w = weights(name)
                o = take(name)
                for t in range(NT):
                    for c in range(nk):
                        ins = mm(o[:, t * GW:(t + 1) * GW], lhs[:, c, t * P:(t + 1) * P], w[:, c, :],
                                 start=(t == 0 and c == 0), stop=(c == nk - 1), skip_group_check=True)
                done(name, ins)

            def many(name, parts):
                o = take(name)
                for n, (lo, hi, lhs, rhs) in enumerate(parts):
                    ins = mm(o[0:lhs.shape[-1], lo:hi], lhs, rhs, start=True, stop=True,
                             skip_group_check=True)
                done(name, ins)

            pe.wait_ge(E("ident_in"), 16)
            for t in range(NT):
                pe.wait_ge(E(f"x_in{t}"), 16)
                for h in range(2):
                    many(f"xT{t}{h}", [(q * P, q * P + P, XTOK[:, t, (4 * h + q) * P:(4 * h + q + 1) * P], ident)
                                       for q in range(4)])
            for t in range(NT):
                for h in range(2):
                    moved(pe, f"xT{t}{h}")
            proj("gq0")
            pe.wait_ge(E("vec_in"), 16 * 9)
            many("vec", [(0, P, VR, ident)])
            pe.wait_ge(E("wsm_in"), 16 * 4)
            o = take("small")
            for c in range(KD):
                ins = mm(o[:, 0:S], WSM[:, c, :], XT[:, c, :], start=(c == 0), stop=(c == KD - 1))
            done("small", ins)
            for n in range(1, 6):
                proj(f"gq{n}")
            pe.wait_ge(E("planes_in"), 16)
            for n in range(2):
                proj(f"lx{n}")
            pe.wait_ge(E("rows_ready"), 1)
            pe.wait_ge(E("rows_ready_act"), 3)
            many("rc", [(t * S + k * P, t * S + k * P + P, r[:, t * P:(t + 1) * P], ident)
                        for t in range(NT) for k, r in enumerate((RW, RX))])
            pe.wait_ge(E("squares"), 2)
            for n in (2, 3, 0, 1):
                many(f"ss{n}", [(0, 512, CM[:, K_BLK], SQ[:, 2 * n:2 * n + 2, :])])
            for n in range(2, 4):
                proj(f"lx{n}")
            for n in range(2):
                o = take(f"bb{n}")
                for m in range(2):
                    for a in range(2):
                        ins = mm(o[64 * a:64 * a + 64, m * S:m * S + S],
                                 ident[:, 96 + 4 * n + 2 * m + a:97 + 4 * n + 2 * m + a].to_broadcast([P, 64]),
                                 RW, start=True, stop=True, skip_group_check=True)
                done(f"bb{n}", ins)
            for n in range(2):
                o = take(f"gb{n}")
                for m in range(2):
                    for a in range(2):
                        ins = mm(o[64 * a:64 * a + 64, m * S:m * S + S],
                                 ident[:, 64 + 4 * n + 2 * m + a:65 + 4 * n + 2 * m + a].to_broadcast([P, 64]),
                                 RW, start=True, stop=True, skip_group_check=True)
                done(f"gb{n}", ins)
            proj("ly0")
            pe.wait_ge(E("gsilu_v"), 1)
            for t in range(NT):
                many(f"vt{t}", [(j * P, j * P + P, GCO[:, 8 + j, t * P:(t + 1) * P], ident) for j in range(GP)])
            pe.wait_ge(E("khat"), 1)
            for t in range(NT):
                many(f"kt{t}", [(j * P, j * P + P, KT[:, j, t * P:(t + 1) * P], ident) for j in range(GP)])
            for n in range(4):
                many(f"gr{n}", [(m * S, m * S + S, ident[:, 64 + 2 * n + m:65 + 2 * n + m].to_broadcast([P, P]), RW)
                                for m in range(2)])
            proj("ly1")
            for name, R, ready in (("at", KB, "kb_ready"), ("pt", QB, "qb_ready")):
                pe.wait_ge(E(ready), 1)
                for n in range(4):
                    t = n // 2
                    many(f"{name}{n}", [(m * S, m * S + S, KT[:, 2 * (n % 2) + m, t * P:(t + 1) * P],
                                         R[:, 2 * (n % 2) + m, :, t * P:(t + 1) * P]) for m in range(2)])
                proj("ly2" if name == "at" else "ly3")
            for n in range(4):
                pe.wait_ge(E("xt1"), n + 1)
                many(f"x1{n}", [(q * P, q * P + P, XTi[:, n, q * P:(q + 1) * P], ident) for q in range(4)])

            def fill(slot):
                for name in FILL[slot]:
                    if name == "lg":
                        w = weights("lg7").rearrange("p c n -> p (c n)").rearrange("p (k b n) -> p k b n",
                                                                                   k=2, b=NB)
                        pe.wait_ge(E("xa_ready"), 1)
                        for b in range(NB):
                            many(f"lg{b}", [(k * S, k * S + S, w[:, k, b, :], XA[:, b, :]) for k in range(2)])
                    elif name[:2] == "mr":
                        n = int(name[2])
                        many(name, [(m * S, m * S + S,
                                     ident[:, 2 * n + m:2 * n + m + 1].to_broadcast([P, P]), NM)
                                    for m in range(2)])
                    elif name[:2] == "ms":
                        j = int(name[2])
                        if name == "ms00":
                            moved(pe, "mq")
                            moved(pe, "mk")
                        if name[3] == "0":
                            many(name, [(0, 512, MK[:, j, 0:P], QM[:, j, :, :])])
                        else:
                            many(name, [(0, 256, MK[:, j, P:2 * P], QM[:, j, :, P:2 * P])])
                    elif name == "mn":
                        pe.wait_ge(E("ms_ready"), 1)
                        for n in range(2):
                            moved(pe, f"mv{n}")
                        for t in range(NT):
                            for j in range(2):
                                o = take(f"mn{t}{j}")
                                for a in range(2):
                                    h = 2 * j + a
                                    blocks = [(0, 0)] if t == 0 else [(1, 0), (2, 1)]
                                    for n, (b, s) in enumerate(blocks):
                                        ins = mm(o[:, a * 129:a * 129 + 129], ME[:, h, b, :], V1[:, s, h, :],
                                                 start=(n == 0 and a == 0), stop=(n == len(blocks) - 1),
                                                 skip_group_check=True)
                                done(f"mn{t}{j}", ins)
                    elif name == "mt":
                        for t in range(NT):
                            pe.wait_ge(E("mn_norm"), t + 1)
                            many(f"mt{t}", [(h * P, h * P + P, MN[:, t, h, :], ident) for h in range(MH)])
                    elif name[:2] == "mv":
                        proj_tok(name, XT)
                    else:
                        proj(name)
            for k in range(1, 6):
                for n in range(4):
                    moved(pe, f"x1{n}" if k == 1 else f"t{k - 1}{n}")
                    many(f"y{k}{n}", [(q * P, q * P + P, AT[:, n, q * P:(q + 1) * P], X_[:, n, q * P:(q + 1) * P])
                                      for q in range(4)])
                fill(2 * k - 2)
                if k < 5:
                    for n in range(4):
                        moved(pe, f"y{k}{n}")
                        many(f"z{k}{n}", [(q * P, q * P + P, XTi[:, n, q * P:(q + 1) * P],
                                           Y_[:, n, q * P:(q + 1) * P]) for q in range(4)])
                for n in range(4):
                    moved(pe, f"y{k}{n}")
                    many(f"t{k}{n}", [(q * P, q * P + P, Y_[:, n, q * P:(q + 1) * P],
                                       XTi[:, n, q * P:(q + 1) * P]) for q in range(4)])
                fill(2 * k - 1)
            for n in range(4):
                moved(pe, f"t5{n}")
            for t in range(NT):
                many(f"u{t}", [(h * GK, h * GK + GK, XTi[:, 2 * t + h // 4, (h % 4) * P:(h % 4 + 1) * P],
                                BV[:, t, h * GK:(h + 1) * GK]) for h in range(GH)])
            for t in range(NT):
                o = take(f"w{t}")
                for h in range(GH):
                    a = 64 * (h % 2)
                    ins = mm(o[a:a + 64, (h // 2) * P:(h // 2 + 1) * P], KBE[:, t, h * GK:(h + 1) * GK],
                             XTi[:, 2 * t + h // 4, (h % 4) * P:(h % 4 + 1) * P], start=True, stop=True,
                             skip_group_check=True)
                done(f"w{t}", ins)
            items = branch_items()[1:]
            ready = {0: "ha_ready", 1: "hb_ready", 2: "hc_ready"}

            def branch():
                kind, n, d = items.pop(0)
                if kind == "ga":
                    proj(f"ga{n}{d}")
                else:
                    if d == 0:
                        pe.wait_ge(E(ready[n]), 1)
                    proj(f"br{n}{d}", (LY, HB, HC)[n], (8, 4, 4)[n])
            branch()
            for c in range(NC):
                t, a = c // 2, 64 * (c % 2)
                pe.wait_ge(E("state"), c + 1)
                moved(pe, f"w{t}")
                o = take(f"ws{c}")
                for j in range(GP):
                    ins = mm(o[a:a + 64, j * P:(j + 1) * P], WT[:, t, j, a:a + 64], ST[:, j * P:(j + 1) * P],
                             start=True, stop=True, skip_group_check=True)
                done(f"ws{c}", ins)
                branch()
                oo = take(f"o{t}") if c % 2 == 0 else ps(f"o{t}")
                for j in range(GP):
                    mm(oo[a:a + 64, j * P:(j + 1) * P], QG[:, j, c * CH:(c + 1) * CH], ST[:, j * P:(j + 1) * P],
                       start=(j == 0), stop=False, skip_group_check=True)
                moved(pe, f"ws{c}")
                if c < NC - 1:
                    o = take(f"sn{c}")
                    for j in range(GP):
                        ins = mm(o[:, j * P:(j + 1) * P], KDE[a:a + 64, t, j * P:(j + 1) * P],
                                 DE[a:a + 64, t, j * P:(j + 1) * P], start=True, stop=True,
                                 skip_group_check=True)
                    done(f"sn{c}", ins)
                for h in range(GH):
                    q = (h % 4) * P + a
                    ins = mm(oo[a:a + 64, h * GK:(h + 1) * GK], PT[a:a + 64, 2 * t + h // 4, q:q + 64],
                             DE[a:a + 64, t, h * GK:(h + 1) * GK], start=False, stop=True, skip_group_check=True)
                if c % 2 == 1:
                    done(f"o{t}", ins)
                branch()
            for t in range(NT):
                branch()
                branch()
                pe.wait_ge(E("o_norm"), t + 1)
                many(f"ot{t}", [(j * P, j * P + P, OQ[:, t, j * P:(j + 1) * P], ident) for j in range(GP)])
            while items:
                branch()
            def out_proj(t, h):
                o = take(f"wo{t}{h}")
                for d in range(2):
                    if 2 * h + d == 3:
                        pe.wait_ge(E("wo3_in"), 16)
                        w = WO3
                    else:
                        w = weights(f"wo{2 * h + d}")
                    for c in range(KD):
                        if (t, h, d, c % 2) == (0, 0, 0, 0):
                            pe.wait_ge(E("merged"), c // 2 + 1)
                        ins = mm(o[:, d * GW:(d + 1) * GW], MG[:, c, t * P:(t + 1) * P], w[:, c, :],
                                 start=(d == 0 and c == 0), stop=(c == KD - 1), skip_group_check=True)
                done(f"wo{t}{h}", ins)

            def turn_x1(t):
                pe.wait_ge(E("x1_ready"), t + 1)
                for h in range(2):
                    many(f"x1T{t}{h}", [(q * P, q * P + P, X1[:, t, (4 * h + q) * P:(4 * h + q + 1) * P], ident)
                                        for q in range(4)])

            def logits(t):
                o = take(f"lgt{t}")
                for c in range(KD):
                    if c % 4 == 0:
                        moved(pe, f"x1T{t}{c // 4}")
                    ins = mm(o[:, 0:NE], X1T[:, c, t * P:(t + 1) * P], ROUT[:, c, :], start=(c == 0),
                             stop=(c == KD - 1))
                done(f"lgt{t}", ins)

            def residual(t, h):
                b = 4 + 2 * t + h
                pe.wait_ge(E(f"bank_free{b}"), bank_total[b])
                mm(PS[:, b, :], AID, X1[:, t, h * 512:(h + 1) * 512], start=True, stop=False,
                   skip_group_check=True)
            out_proj(0, 0)
            out_proj(0, 1)
            out_proj(1, 0)
            turn_x1(0)
            out_proj(1, 1)
            pe.wait_ge(E("rout_in"), 32)
            logits(0)
            residual(0, 0)
            residual(0, 1)
            turn_x1(1)
            logits(1)
            pe.wait_ge(E("sel_ready"), 1)
            o = take("cnt")
            mm(o[:, 0:32], CM[:, K_BEFORE], SEL[:, 0, :], start=True, stop=True, skip_group_check=True)
            mm(o[:, 32:64], CM[:, K_ONES], SEL[:, 0, :], start=False, stop=False, skip_group_check=True)
            mm(o[:, 64:96], CM[:, K_ONES], SEL[:, 0, :], start=False, stop=False, skip_group_check=True)
            pe.wait_ge(E("sel_ready"), 2)
            mm(o[:, 32:64], CM[:, K_BEFORE], SEL[:, 1, :], start=False, stop=True, skip_group_check=True)
            ins = mm(o[:, 64:96], CM[:, K_ONES], SEL[:, 1, :], start=False, stop=True, skip_group_check=True)
            done("cnt", ins)
            residual(1, 0)

            def scatter(event):
                for t in range(NT):
                    for a in range(2):
                        ins = mm(PS[:, 4 + 2 * t + a, :], GTS[64 * a:64 * a + CAP, t * P:(t + 1) * P],
                                 YS[64 * a:64 * a + CAP, :], start=False, stop=False, skip_group_check=True)
                    if event:
                        ins.then_inc(E(event), 1)

            def gather():
                for t in range(NT):
                    for a in range(2):
                        ins = mm(PS[64 * a:64 * a + CAP, 2, :], ONE[:, t, :], X1[:, t, a * 512:(a + 1) * 512],
                                 start=(t == 0), stop=(t == NT - 1), skip_group_check=True)
                return ins

            def transpose(bank, src):
                for q in range(4):
                    ins = mm(PS[:, bank, q * P:(q + 1) * P], src[:, q * P:(q + 1) * P], ident,
                             start=True, stop=True, skip_group_check=True)
                return ins

            for b in range(4):
                if b != 3:
                    pe.wait_ge(E(f"bank_free{b}"), bank_total[b])
            pe.wait_ge(E("onehot"), 1)
            gather().then_inc(E("xg_full"), 1)
            pe.wait_ge(E("gates_ready"), 1)
            o = take("gT")
            for a in range(2):
                for t in range(NT):
                    ins = mm(o[64 * a:64 * a + NE, t * P:(t + 1) * P], GAT[:, t, 0:NE], ident, start=True,
                             stop=True, skip_group_check=True)
            done("gT", ins)
            pe.wait_ge(E("xg_ready"), 1)
            transpose(2, XG).then_inc(E("xe_full"), 1)
            residual(1, 1)
            pe.wait_ge(E("b1r_in"), 16)
            pe.wait_ge(E("rounds_ready"), 1)
            rounds = pe.value_load(NR[0:1, 0:1], min_val=1, max_val=ROUNDS)

            def expert(turn, j):
                i = turn * EB + j

                def chunk(c):
                    n = j * EC + c
                    pe.wait_ge(E(f"chunk_in{n % SLOTS}"), 16 * (EB * EC // SLOTS) * turn + 16 * (n // SLOTS) + 16)
                    return SLOT[n % SLOTS]
                pe.wait_ge(E("pick"), i + 1)
                for b in range(2):
                    for a in range(2):
                        mm(PS[64 * a:64 * a + CAP, b, :], PICK[0:NE, :],
                           B1R[0:NE, b * FF + a * 512:b * FF + a * 512 + 512], start=True, stop=False,
                           skip_group_check=True)
                pe.wait_ge(E("xe_ready"), i + 1)
                for c in range(KD):
                    w = chunk(c)
                    for b in range(2):
                        for a in range(2):
                            ins = mm(PS[64 * a:64 * a + CAP, b, :], XE[:, c % 4, 64 * (c // 4):64 * (c // 4) + CAP],
                                     w[:, b * FF + a * 512:b * FF + a * 512 + 512], start=False,
                                     stop=(c == KD - 1), skip_group_check=True)
                    ins.then_inc(E("chunk_used"), 1)
                    if c == 1:
                        pe.wait_ge(E("ys_ready"), i + 1)
                        scatter(None)
                    if c == 4:
                        pe.wait_ge(E("gated"), i + 1)
                        for t in range(NT):
                            ins = mm(PS[:, 3, t * P:(t + 1) * P], GAD[:, t, :], ident, start=True, stop=True,
                                     skip_group_check=True)
                        ins.then_inc(E("gt_full"), 1)
                pe.wait_ge(E("onehot"), i + 2)
                gather().then_inc(E("xg_full"), 1)
                pe.wait_ge(E("gt_ready"), i + 1)
                pe.wait_ge(E("hid_ready"), i + 1)
                transpose(3, HID).then_inc(E("ht_full"), 1)
                pe.wait_ge(E("xg_ready"), i + 2)
                transpose(2, XG).then_inc(E("xe_full"), 1)
                pe.wait_ge(E("ht_ready"), i + 1)
                for c in range(KF):
                    if c % 2 == 0:
                        w = chunk(KD + c // 2).rearrange("p (c n) -> p c n", n=D)
                    for a in range(2):
                        ins = mm(PS[64 * a:64 * a + CAP, 3, :], HT[:, c % 4, 64 * (c // 4):64 * (c // 4) + CAP],
                                 w[:, c % 2, a * 512:(a + 1) * 512], start=(c == 0), stop=(c == KF - 1),
                                 skip_group_check=True)
                    if c % 2:
                        ins.then_inc(E("chunk_used"), 1)
            with pe.Fori(0, rounds) as r, pe.Fori(0, NE // EB) as q:
                for j in range(EB):
                    expert(r * (NE // EB) + q, j)
            pe.wait_ge(E("ys_ready"), rounds * NE + 1)
            scatter("acc_done")

        @block.scalar
        def _(act):
            tick = [0]

            def step(ins):
                tick[0] += 1
                ins.then_inc(E("act_own"), 1)
                act.wait_ge(E("act_own"), tick[0])

            A = nc_s.activation
            act.dma_start(ident, planes[:, 0:P]).then_inc(E("ident_in"), 16)
            act.dma_start(CM[:, 1:], planes[:, P:].rearrange("p (k n) -> p k n", n=P)).then_inc(E("planes_in"), 16)
            for h in range(2):
                full(act, f"xT1{h}")
                nc_s.copy(XT[:, 4 * h:4 * h + 4, P:2 * P], ps(f"xT1{h}").rearrange("p (c s) -> p c s", s=P)
                          ).then_inc(free(f"xT1{h}"), 1)
            act.wait_ge(E("small_zero"), 4)
            for row, src in ((V_CW, lru_conv_w[0].rearrange("w (b p) -> (w b) p", p=P)),
                             (V_CB, lru_conv_b[0].rearrange("(b p) -> b p", p=P)),
                             (V_BA, lru_ba[0]), (V_BX, lru_bx[0]),
                             (V_LAM, lru_lambda[0].rearrange("(b p) -> b p", p=P)),
                             (V_GCW, gd_conv_w[0].rearrange("w (b p) -> (w b) p", p=P)),
                             (V_MG, ml_norm_g[0])):
                act.dma_start(VR[row:row + src.shape[0], :], src).then_inc(E("vec_in"), 16)
            for a in range(2):
                act.dma_start(VR[V_GG:V_GG + 1, 64 * a:64 * a + 64], gd_norm_g[0:1, :]).then_inc(E("vec_in"), 16)

            def evac(name, dst, func=None):
                full(act, name)
                src = ps(name).rearrange("p (c s) -> p c s", s=S)
                if func is None:
                    ins = nc_s.copy(dst, src)
                else:
                    ins = A(dst, src, func)
                ins.then_inc(free(name), 1)
            for row, dst, src in ((0, BIAS, ml_i_bias), (32, BIAS, ml_f_bias), (64, BIAS, gd_dt_bias),
                                  (64, ALOG, gd_a_log)):
                n = src.shape[1]
                act.dma_start(dst[row:row + n, :], src.rearrange("a n -> n a")).then_inc(E("bias_in"), 16)
            act.dma_start(ROUT, router_w[0].rearrange("(c p) e -> p c e", p=P)).then_inc(E("rout_in"), 16)
            act.dma_start(RBIAS, router_b[0].partition_broadcast(P)).then_inc(E("rout_in"), 16)
            act.wait_ge(E("gin_pad"), 1)
            evac("gq0", GIN[:, 0:2, 3:])
            full(act, "vec")
            nc_s.copy(VC, ps("vec")[:, 0:P]).then_inc(free("vec"), 1)
            act.wait_ge(E("planes_in"), 16)
            act.wait_ge(E("bias_in"), 64)
            step(A(ALOG, ALOG, ACT.Exp))
            nc_s.mul(COEF, ALOG, CM[:, K_COLS, 1:2]).then_inc(E("coef"), 1)
            moved(act, "vec")
            A(TS[:, 0:8], VC[:, V_LAM:V_LAM + 8], ACT.Abs).then_inc(E("lam_abs"), 1)
            act.wait_ge(E("lam_abs"), 1)
            A(TS[:, 0:8], TS[:, 0:8], ACT.Exp, scale=-1.0).then_inc(E("lam_exp"), 1)

            act.wait_ge(E("row_abs"), 1)
            A(ROWT[3], ROWT[2], ACT.Exp, scale=-1.0).then_inc(E("row_exp"), 1)
            evac("gq1", GIN[:, 2:4, 3:])
            act.wait_ge(E("row_scan"), 1)
            nc_s.copy(ROWT[7][0:32], RB[32:64]).then_inc(E("row_b0"), 1)
            nc_s.copy(RW[64:96], RB[64:96]).then_inc(E("rows_ready_act"), 1)
            A(RW[96:128], ROWT[0][96:128], ACT.Sigmoid).then_inc(E("rows_beta"), 1)
            evac("gq2", GIN[:, 4:6, 3:])
            act.wait_ge(E("row_mb"), 1)
            A(RW[32:64], ROWT[6][0:32], ACT.Exp, scale=-1.0).then_inc(E("rows_ready_act"), 1)
            act.wait_ge(E("rx_zero"), 1)
            act.wait_ge(E("row_kd"), 1)
            A(RX[64:96], ROWT[5][64:96], ACT.Exp).then_inc(E("rows_ready_act"), 1)

            def conv_sigmoid(n):
                act.wait_ge(E("gconv"), n + 1)
                A(GSIG[:, 4 * n:4 * n + 4, :], GCO[:, 4 * n:4 * n + 4, :], ACT.Sigmoid).then_inc(E("gsig"), 1)

            def square(n):
                act.wait_ge(E("gsilu_qk"), n + 1)
                A(SQ[:, 4 * n:4 * n + 4, :], GCO[:, 4 * n:4 * n + 4, :], ACT.Square).then_inc(E("squares"), 1)
            evac("gq3", GIN[:, 6:8, 3:])
            conv_sigmoid(0)
            evac("gq4", GIN[:, 8:10, 3:])
            square(0)
            conv_sigmoid(1)
            evac("gq5", GIN[:, 10:12, 3:])
            square(1)
            act.wait_ge(E("lx_pad"), 1)
            evac("lx0", LX[:, 0:2, 3:])
            conv_sigmoid(2)
            evac("lx1", LX[:, 2:4, 3:])
            full(act, "rc")
            nc_s.copy(RC, ps("rc").rearrange("p (t k n) -> p t k n", t=2, k=2)).then_inc(free("rc"), 1)
            act.wait_ge(E("eps_ready"), 1)
            for n in (2, 3, 0, 1):
                full(act, f"ss{n}")
                A(RN[:, 2 * n:2 * n + 2, :], ps(f"ss{n}").rearrange("p (c s) -> p c s", s=S), ACT.Ln,
                  bias=TS[:, 31:32]).then_inc(free(f"ss{n}"), 1)
                if n % 2:
                    moved(act, f"ss{n - 1}")
                    moved(act, f"ss{n}")
                    A(RN[:, 2 * n - 2:2 * n + 2, :], RN[:, 2 * n - 2:2 * n + 2, :], ACT.Exp, scale=-0.5
                      ).then_inc(E("norms"), 1)
            for n in range(2, 4):
                evac(f"lx{n}", LX[:, 2 * n:2 * n + 2, 3:])
            for n in range(2):
                full(act, f"gb{n}")
                A(EG[:, 2 * n:2 * n + 2, :], ps(f"gb{n}").rearrange("p (c s) -> p c s", s=S), ACT.Exp
                  ).then_inc(free(f"gb{n}"), 1)
            moved(act, "rc")
            A(TS[:, 8:24].rearrange("p (t h) -> p t h", t=NT), RC[:, :, 0, 64:72], ACT.Exp).then_inc(E("egc"), 1)
            evac("ly0", LY[:, 0:2, :])
            for n in range(4):
                act.wait_ge(E("gam_arg"), n + 1)
                A(GAM[:, n, :], GAM[:, n, :], ACT.Exp).then_inc(E("gam"), 1)
            for n in range(1, 4):
                evac(f"ly{n}", LY[:, 2 * n:2 * n + 2, :])
            for n in range(4):
                full(act, f"x1{n}")
                nc_s.copy(X_[:, n, :], ps(f"x1{n}")).then_inc(free(f"x1{n}"), 1)
            act.wait_ge(E("qm_zero"), 2)
            full(act, "mq")
            nc_s.mul(QM[0:64, :, 0, :], ps("mq")[0:64].rearrange("p (c s) -> p c s", s=S), MQ ** -0.5)
            nc_s.mul(QM[64:128, :, 1, :], ps("mq")[64:128].rearrange("p (c s) -> p c s", s=S), MQ ** -0.5
                     ).then_inc(free("mq"), 1)
            evac("mk", MK)
            act.wait_ge(E("gelu_arg"), 1)
            A(LU, LU, ACT.Tanh, scale=0.7978845608028654).then_inc(E("gelu_tanh"), 1)
            act.wait_ge(E("lx_free"), 1)
            moved(act, "pt3")
            for b in range(NB):
                if b == 4:
                    for n in range(2):
                        act.wait_ge(E("me_arg"), n + 1)
                        A(ME[:, 2 * n:2 * n + 2, :, :], ME[:, 2 * n:2 * n + 2, :, :], ACT.Exp
                          ).then_inc(E("me"), 1)
                full(act, f"lg{b}")
                A(LR[:, b, :], ps(f"lg{b}")[:, 0:S], ACT.Sigmoid, bias=VC[:, V_BA + b:V_BA + b + 1])
                A(LG[:, b, :], ps(f"lg{b}")[:, S:2 * S], ACT.Sigmoid, bias=VC[:, V_BX + b:V_BX + b + 1]
                  ).then_inc(free(f"lg{b}"), 1)
            for b in range(NB - 4, NB):
                moved(act, f"lg{b}")
            act.sem_inc(E("lgates"), 1)
            act.wait_ge(E("v1_one"), 1)

            def evac_v(n):
                full(act, f"mv{n}")
                nc_s.copy(V1[:, :, 2 * n:2 * n + 2, 0:128],
                          ps(f"mv{n}").rearrange("p (t h e) -> p t h e", t=NT, h=2)).then_inc(free(f"mv{n}"), 1)
            act.wait_ge(E("gelu_used"), 1)
            act.wait_ge(E("lsp"), 1)
            for b in range(NB):
                A(LU[:, b, :], LR[:, b, :], ACT.Tanh, scale=LSP[:, b:b + 1])
                ins = A(LR[:, b, :], LR[:, b, :], ACT.Exp, scale=NLSP[:, b:b + 1])
            ins.then_inc(E("la"), 1)
            evac_v(0)
            evac_v(1)
            act.wait_ge(E("lu_arg"), 1)
            A(LU, LU, ACT.Sqrt).then_inc(E("lu"), 1)
            evac("mo0", MO[:, 0:2, :], func=ACT.Sigmoid)
            for t in range(NT):
                act.wait_ge(E("mn_scaled"), t + 1)
                for h in range(MH):
                    ins = A(MSQ[:, t, h, :], MN[:, t, h, :], ACT.Square,
                            accum_out=RT2[:, 4 * t + h:4 * t + h + 1])
                ins.then_inc(E("mss"), 1)
                act.wait_ge(E("mss"), 2 * t + 1)
                A(RT2[:, 8 + 4 * t:12 + 4 * t], RT2[:, 4 * t:4 * t + 4], ACT.Sqrt, bias=TS[:, 31:32],
                  scale=1.0 / MV).then_inc(E("mss"), 1)
            evac("mo1", MO[:, 2:4, :], func=ACT.Sigmoid)
            for n in range(2):
                full(act, f"gz{n}")
                A(GZ[:, 2 * n:2 * n + 2, :], ps(f"gz{n}").rearrange("p (c s) -> p c s", s=S), ACT.Sigmoid
                  ).then_inc(E("zsig"), 1)
            gates = [f"{n}{d}" for kind, n, d in branch_items() if kind == "ga"]

            def gate(k):
                full(act, f"ga{gates[k]}")
                if k >= 4:
                    moved(act, f"br{gates[k - 4]}")
                A(SG[k % 4], ps(f"ga{gates[k]}"), ACT.Sigmoid).then_inc(free(f"ga{gates[k]}"), 1)

            def o_root(t):
                act.wait_ge(E("oss"), t + 1)
                A(TS[:, 8 * t:8 * t + 8], TS[:, 8 * t:8 * t + 8], ACT.Sqrt, bias=TS[:, 31:32], scale=1.0 / GK
                  ).then_inc(E("osq"), 1)
            act.wait_ge(E("ha_ready"), 1)
            gate(0)
            for t in range(NT):
                full(act, f"u{t}")
                nc_s.copy(U_[:, t, :], ps(f"u{t}")).then_inc(free(f"u{t}"), 1)
            for t in range(NT):
                full(act, f"w{t}")
                nc_s.copy(WT[:, t, :, :], ps(f"w{t}").rearrange("p (j n) -> p j n", j=GP)).then_inc(free(f"w{t}"), 1)
            for k in range(1, 4):
                gate(k)
            o_root(0)
            gate(4)
            gate(5)
            o_root(1)
            for k in range(6, 12):
                gate(k)
                if k == 8:
                    act.wait_ge(E("hb_ready"), 1)
                    act.wait_ge(E("hc_ready"), 1)
                    act.dma_start(LNG, ln1_g[0].partition_broadcast(P)).then_inc(E("ln1_in"), 16)
                    act.dma_start(LNB, ln1_b[0].partition_broadcast(P)).then_inc(E("ln1_in"), 16)

            act.wait_ge(E("merged"), 4)
            act.dma_start(B1R[0:NE, :], exp_b1[0]).then_inc(E("b1r_in"), 16)
            act.wait_ge(E("ys_zero"), 1)
            for a in range(2):
                act.dma_start(YS[64 * a:64 * a + NE, :], exp_b2[0, :, a * 512:(a + 1) * 512]
                              ).then_inc(E("b2_in"), 16)

            def deviation(n, t):
                act.wait_ge(E(f"ln{n}_var"), t + 1)
                A(TS[:, 8 + t:9 + t], TS[:, 8 + t:9 + t], ACT.Sqrt, bias=TS[:, 30:31]).then_inc(E(f"ln{n}_sd"), 1)
            for t in range(NT):
                deviation(1, t)
                for h in range(2):
                    full(act, f"x1T{t}{h}")
                    nc_s.copy(X1T[:, 4 * h:4 * h + 4, t * P:(t + 1) * P],
                              ps(f"x1T{t}{h}").rearrange("p (c s) -> p c s", s=P)).then_inc(free(f"x1T{t}{h}"), 1)
            act.dma_start(LNG, ln2_g[0].partition_broadcast(P)).then_inc(E("ln2_in"), 16)
            act.dma_start(LNB, ln2_b[0].partition_broadcast(P)).then_inc(E("ln2_in"), 16)
            act.wait_ge(E("exl_arg"), 2)
            A(EXL, EXL, ACT.Exp).then_inc(E("exl"), 1)
            act.wait_ge(E("xg_full"), 1)
            nc_s.copy(XG, PS[:, 2, :]).then_inc(E("xg_ready"), 1)
            full(act, "gT")
            for a in range(2):
                h = slice(64 * a, 64 * a + NE)
                ins = nc_s.copy(GTS[h, :], ps("gT")[h, 0:S])
            ins.then_inc(free("gT"), 1)
            act.wait_ge(E("xe_full"), 1)
            nc_s.copy(XE, PS[:, 2, :].rearrange("p (q n) -> p q n", q=4)).then_inc(E("xe_ready"), 1)
            act.wait_ge(E("b2_in"), 32)
            moved(act, "gT")
            act.sem_inc(E("ys_ready"), 1)
            act.wait_ge(E("rounds_ready"), 1)
            rounds = act.value_load(NR[0:1, 0:1], min_val=1, max_val=ROUNDS)
            with act.Fori(0, rounds) as r, act.Fori(0, NE) as e:
                i = r * NE + e
                act.wait_ge(E("gt_full"), i + 1)
                nc_s.copy(GTS, PS[:, 3, 0:S]).then_inc(E("gt_ready"), 1)
                act.wait_ge(E("glu_ready"), i + 1)
                A(SIG, GLU, ACT.Sigmoid, scale=SWIGLU).then_inc(E("sig_ready"), 1)
                act.wait_ge(E("xg_full"), i + 2)
                nc_s.copy(XG, PS[:, 2, :]).then_inc(E("xg_ready"), 1)
                act.wait_ge(E("xe_full"), i + 2)
                nc_s.copy(XE, PS[:, 2, :].rearrange("p (q n) -> p q n", q=4)).then_inc(E("xe_ready"), 1)
                act.wait_ge(E("chunk_used"), EC * i + EC)
                nc_s.copy(YS, PS[:, 3, :]).then_inc(E("ys_ready"), 1)
            for t in range(NT):
                deviation(2, t)

        @block.vector
        def _(dve):
            tick = [0]

            def step(ins):
                tick[0] += 1
                ins.then_inc(E("dve_own"), 1)
                dve.wait_ge(E("dve_own"), tick[0])

            tt, ts, stt = nc_v.tensor_tensor, nc_v.tensor_scalar, nc_v.scalar_tensor_tensor

            def softplus_tail(y, e, out, t1, t2, t3):
                step(ts(t1, e, 2.0, None, ALU.add))
                step(nc_v.reciprocal(t1, t1))
                step(tt(t1, t1, e, ALU.mult))
                step(tt(t2, t1, t1, ALU.mult))
                step(ts(t3, t2, 1.0 / 15, None, ALU.mult))
                for n in (13, 11, 9, 7, 5, 3):
                    step(stt(t3, t3, 1.0 / n, t2, ALU.add, ALU.mult))
                step(stt(t3, t3, 1.0, t1, ALU.add, ALU.mult))
                step(ts(t1, y, 0.0, None, ALU.max))
                step(stt(out, t3, 2.0, t1, ALU.mult, ALU.add))

            for h in range(2):
                full(dve, f"xT0{h}")
                nc_v.tensor_copy(XT[:, 4 * h:4 * h + 4, 0:P], ps(f"xT0{h}").rearrange("p (c s) -> p c s", s=P)
                                 ).then_inc(free(f"xT0{h}"), 1)
            dve.wait_ge(E("ident_in"), 16)
            dve.wait_ge(E("planes_in"), 16)
            nc_v.memset(TS[:, 30:31], LN_EPS)
            nc_v.memset(TS[:, 31:32], RMS_EPS).then_inc(E("eps_ready"), 1)
            moved(dve, "vec")
            dve.wait_ge(E("lam_exp"), 1)
            step(ts(TS[:, 8:16], VC[:, V_LAM:V_LAM + 8], -1.0, None, ALU.mult))
            softplus_tail(TS[:, 8:16], TS[:, 0:8], TS[:, 0:8], TS[:, 16:24], LSP, NLSP)
            step(ts(LSP, TS[:, 0:8], LRU_C, None, ALU.mult))
            ts(NLSP, TS[:, 0:8], -LRU_C, None, ALU.mult).then_inc(E("lsp"), 1)
            full(dve, "small")
            dve.wait_ge(E("bias_in"), 64)
            dve.wait_ge(E("coef"), 1)
            PRE, YR, AB, EX, SPT, L2, MB, B0 = ROWT
            ts(PRE, ps("small")[:, 0:S], BIAS, None, ALU.add).then_inc(free("small"), 1)
            dve.wait_ge(free("small"), 1)
            step(ts(YR, PRE, CM[:, K_COLS, 0:1], None, ALU.mult))
            stt(AB, YR, -1.0, YR, ALU.mult, ALU.max).then_inc(E("row_abs"), 1)
            dve.wait_ge(E("row_exp"), 1)
            softplus_tail(YR, EX, SPT, L2, MB, B0)
            step(ts(SPT, SPT, COEF, None, ALU.mult))
            nc_v.tensor_tensor_scan(RB, CM[:, K_RST0:K_RST1 + 1, :].rearrange("p a b -> p (a b)"), SPT, 0.0,
                                    ALU.mult, ALU.add).then_inc(E("row_scan"), 1)

            def rows():
                dve.wait_ge(E("row_scan"), 1)
                dve.wait_ge(E("row_b0"), 1)
                step(tt(RW[0:32], PRE[0:32], B0[0:32], ALU.subtract))
                step(nc_v.tensor_tensor_scan(SPT[0:32], RW[0:32], RW[0:32], 0.0, ALU.max, ALU.max))
                tt(MB[0:32], SPT[0:32], B0[0:32], ALU.add).then_inc(E("row_mb"), 1)
                dve.wait_ge(E("nm_zero"), 1)
                step(ts(NM[0:32], SPT[0:32], -1.0, None, ALU.mult))
                g4 = RB[64:96].rearrange("p (c l) -> p c l", l=CH)
                tt(L2[64:96].rearrange("p (c l) -> p c l", l=CH), g4[:, :, CH - 1:CH].to_broadcast([32, NC, CH]),
                   g4, ALU.subtract).then_inc(E("row_kd"), 1)
                dve.wait_ge(E("row_kd"), 1)
                dve.wait_ge(E("rows_beta"), 1)
                dve.sem_inc(E("rows_ready"), 1)

            def conv(dst, src, w0, nb, b, bias=None):
                taps = [VC[:, w0 + nb * j + b:w0 + nb * j + b + 1] for j in range(4)]
                if bias is None:
                    step(ts(dst, src[:, b, 0:S], taps[0], None, ALU.mult))
                else:
                    step(ts(dst, src[:, b, 0:S], taps[0], bias, ALU.mult, ALU.add))
                for j in range(1, 4):
                    ins = stt(dst, src[:, b, j:j + S], taps[j], dst, ALU.mult, ALU.add)
                    step(ins)

            def silu(n):
                dve.wait_ge(E("gsig"), n + 1)
                step(tt(GCO[:, 4 * n:4 * n + 4, :], GCO[:, 4 * n:4 * n + 4, :], GSIG[:, 4 * n:4 * n + 4, :],
                        ALU.mult))
                dve.sem_inc(E("gsilu_qk" if n < 2 else "gsilu_v"), 1)
            for n in range(6):
                moved(dve, f"gq{n}")
                for b in (2 * n, 2 * n + 1):
                    conv(GCO[:, b, :], GIN, V_GCW, 12, b)
                if n % 2:
                    dve.sem_inc(E("gconv"), 1)
                if n == 0:
                    rows()
                if n in (2, 4):
                    silu(n // 2 - 1)
            silu(2)
            dve.sem_inc(E("gsilu"), 1)

            def conv_lru(n):
                moved(dve, f"lx{n}")
                for b in (2 * n, 2 * n + 1):
                    conv(XA[:, b, :], LX, V_CW, 8, b, VC[:, V_CB + b:V_CB + b + 1])
            conv_lru(0)
            dve.wait_ge(E("qb_zero"), 4)
            dve.wait_ge(E("norms"), 1)
            step(tt(KT, GCO[:, 4:8, :], RN[:, 4:8, :], ALU.mult))
            dve.sem_inc(E("khat"), 1)
            for n in range(2):
                full(dve, f"bb{n}")
                for a in range(2):
                    h = slice(64 * a, 64 * a + 64)
                    ins = tt(KB[h, 2 * n:2 * n + 2, a, :], ps(f"bb{n}")[h].rearrange("p (c s) -> p c s", s=S),
                             KT[h, 2 * n:2 * n + 2, :], ALU.mult)
                ins.then_inc(free(f"bb{n}"), 1)
                dve.wait_ge(free(f"bb{n}"), uses[f"bb{n}"][1])
            dve.sem_inc(E("kb_ready"), 1)
            dve.wait_ge(E("norms"), 2)
            for a in range(2):
                h = slice(64 * a, 64 * a + 64)
                step(stt(QB[h, :, a, :], GCO[h, 0:4, :], GK ** -0.5, RN[h, 0:4, :], ALU.mult, ALU.mult))
            dve.sem_inc(E("qb_ready"), 1)
            conv_lru(1)
            for n in range(2):
                moved(dve, f"gb{n}")
            for a in range(2):
                h = slice(64 * a, 64 * a + 64)
                step(tt(QG[h], QB[h, :, a, :], EG[h], ALU.mult))
            dve.wait_ge(E("egc"), 1)
            moved(dve, "rc")
            egc = TS[:, 8:24].rearrange("p (t h) -> p t h", t=NT)
            step(tt(BG, egc, RC[:, :, 0, 96:104], ALU.mult))
            for t in range(NT):
                full(dve, f"vt{t}")
                tt(BV[:, t, :].rearrange("p (h e) -> p h e", h=GH), ps(f"vt{t}").rearrange("p (h e) -> p h e", h=GH),
                   RC[:, t, 0, 96:104].unsqueeze(2).to_broadcast([P, GH, GK]), ALU.mult).then_inc(free(f"vt{t}"), 1)
            for t in range(NT):
                full(dve, f"kt{t}")
                k3 = ps(f"kt{t}").rearrange("p (h e) -> p h e", h=GH)
                tt(KBE[:, t, :].rearrange("p (h e) -> p h e", h=GH), k3,
                   BG[:, t, :].unsqueeze(2).to_broadcast([P, GH, GK]), ALU.mult)
                tt(KDE[:, t, :].rearrange("p (h e) -> p h e", h=GH), k3,
                   RC[:, t, 1, 64:72].unsqueeze(2).to_broadcast([P, GH, GK]), ALU.mult).then_inc(free(f"kt{t}"), 1)
                dve.wait_ge(free(f"kt{t}"), uses[f"kt{t}"][1])
            for t in range(NT):
                for h in range(GH):
                    if t == 0 and h % 2 == 0:
                        full(dve, f"gr{h // 2}")
                    ins = stt(GAM[:, 2 * t + h // 4, (h % 4) * P:(h % 4 + 1) * P],
                              ps(f"gr{h // 2}")[:, (h % 2) * S + t * P:(h % 2) * S + (t + 1) * P],
                              RC[:, t, 0, 64 + h:65 + h], CM[:, K_GTRI], ALU.subtract, ALU.add)
                    if t == 1 and h % 2 == 1:
                        ins.then_inc(free(f"gr{h // 2}"), 1)
                    if t == 0 and h % 4 == 3:
                        ins.then_inc(E("gam_arg"), 1)
            for n in range(4):
                dve.wait_ge(free(f"gr{n}"), uses[f"gr{n}"][1])
            dve.sem_inc(E("gam_arg"), 2)
            plane4 = lambda k: CM[:, k].unsqueeze(1).to_broadcast([P, 4, P])
            quad = lambda ap: ap.rearrange("p (q n) -> p q n", q=4)
            for n in range(4):
                full(dve, f"at{n}")
                dve.wait_ge(E("gam"), n + 1)
                tt(AT[:, n, :], ps(f"at{n}"), GAM[:, n, :], ALU.mult).then_inc(free(f"at{n}"), 1)
                dve.wait_ge(free(f"at{n}"), uses[f"at{n}"][1])
                step(tt(quad(XTi[:, n, :]), quad(AT[:, n, :]), plane4(K_L0T), ALU.mult))
                step(tt(quad(XTi[:, n, :]), plane4(K_ID), quad(XTi[:, n, :]), ALU.subtract))
                dve.sem_inc(E("xt1"), 1)
            for n in range(4):
                full(dve, f"pt{n}")
                tt(PT[:, n, :], ps(f"pt{n}"), GAM[:, n, :], ALU.mult).then_inc(free(f"pt{n}"), 1)

            def gelu_argument():
                for n in range(4):
                    moved(dve, f"ly{n}")
                step(tt(LU, LY, LY, ALU.mult))
                step(ts(LU, LU, 0.044715, 1.0, ALU.mult, ALU.add))
                step(tt(LU, LU, LY, ALU.mult))
                dve.sem_inc(E("gelu_arg"), 1)

            def gelu():
                dve.wait_ge(E("gelu_tanh"), 1)
                step(stt(LY, LU, 1.0, LY, ALU.add, ALU.mult))
                dve.sem_inc(E("gelu_used"), 1)

            def lru_input():
                dve.wait_ge(E("lgates"), 1)
                step(tt(XA, LG, XA, ALU.mult))
                dve.wait_ge(E("la"), 1)
                step(tt(LG, LR, LR, ALU.mult))
                step(stt(LU, LG, 1.0, LU, ALU.add, ALU.mult))
                dve.sem_inc(E("lu_arg"), 1)

            def lru_scan(half):
                dve.wait_ge(E("lu"), 1)
                h = slice(4 * half, 4 * half + 4)
                step(tt(XA[:, h, :], XA[:, h, :], LU[:, h, :], ALU.mult))
                for b in range(4 * half, 4 * half + 4):
                    ins = nc_v.tensor_tensor_scan(LG[:, b, :], LR[:, b, :], XA[:, b, :], 0.0, ALU.mult, ALU.add)
                step(ins)
                step(stt(LY[:, h, :], LG[:, h, :], 0.5, LY[:, h, :], ALU.mult, ALU.mult))
                if half:
                    dve.sem_inc(E("ha_ready"), 1)

            def mlstm_exponents():
                for n in range(2):
                    full(dve, f"mr{n}")
                    for m in range(2):
                        h = 2 * n + m
                        row = ps(f"mr{n}")[:, m * S:(m + 1) * S]
                        stt(ME[:, h, 0, :], row[:, 0:P], RC[:, 0, 0, h:h + 1], CM[:, K_MTRI], ALU.add, ALU.add)
                        ts(ME[:, h, 1, :], row[:, P:2 * P], RC[:, 0, 0, h:h + 1], None, ALU.add)
                        ins = stt(ME[:, h, 2, :], row[:, P:2 * P], RC[:, 1, 0, h:h + 1], CM[:, K_MTRI], ALU.add,
                                  ALU.add)
                    ins.then_inc(free(f"mr{n}"), 1)
                    moved(dve, f"mr{n}")
                    dve.sem_inc(E("me_arg"), 1)

            def mlstm_scores():
                dve.wait_ge(E("me"), 2)
                for j in range(2):
                    full(dve, f"ms{j}0")
                    tt(ME[:, 2 * j:2 * j + 2, 0:2, :], ps(f"ms{j}0").rearrange("p (a b n) -> p a b n", a=2, b=2),
                       ME[:, 2 * j:2 * j + 2, 0:2, :], ALU.mult).then_inc(free(f"ms{j}0"), 1)
                for j in range(2):
                    full(dve, f"ms{j}1")
                    tt(ME[:, 2 * j:2 * j + 2, 2, :], ps(f"ms{j}1")[:, 0:256].rearrange("p (a n) -> p a n", a=2),
                       ME[:, 2 * j:2 * j + 2, 2, :], ALU.mult).then_inc(free(f"ms{j}1"), 1)
                for nm in ("ms00", "ms10", "ms01", "ms11"):
                    moved(dve, nm)
                dve.sem_inc(E("ms_ready"), 1)

            def mlstm_divide():
                for t in range(NT):
                    for j in range(2):
                        full(dve, f"mn{t}{j}")
                        o3 = ps(f"mn{t}{j}")[:, 0:258].rearrange("p (a e) -> p a e", a=2)
                        den = RT2[:, 16 + 4 * t + 2 * j:18 + 4 * t + 2 * j]
                        step(nc_v.tensor_copy(den.unsqueeze(2), o3[:, :, 128:129]))
                        step(stt(den, den, -1.0, den, ALU.mult, ALU.max))
                        step(tt(den, den, RC[:, t, 0, 32 + 2 * j:34 + 2 * j], ALU.max))
                        step(nc_v.reciprocal(den, den))
                        for a in range(2):
                            ins = ts(MN[:, t, 2 * j + a, :], o3[:, a, 0:128], den[:, a:a + 1], None, ALU.mult)
                        ins.then_inc(free(f"mn{t}{j}"), 1)
                        moved(dve, f"mn{t}{j}")
                    dve.sem_inc(E("mn_scaled"), 1)

            def mlstm_norm():
                for t in range(NT):
                    dve.wait_ge(E("mss"), 2 * t + 2)
                    step(nc_v.reciprocal(RT2[:, 8 + 4 * t:12 + 4 * t], RT2[:, 8 + 4 * t:12 + 4 * t]))
                    for h in range(MH):
                        ins = ts(MN[:, t, h, :], MN[:, t, h, :], RT2[:, 8 + 4 * t + h:9 + 4 * t + h], None, ALU.mult)
                    ins.then_inc(E("mn_norm"), 1)

            def mlstm_gate():
                for n in range(2):
                    moved(dve, f"mo{n}")
                for h in range(MH):
                    ins = ts(MO[:, h, :], MO[:, h, :], VC[:, V_MG + h:V_MG + h + 1], None, ALU.mult)
                step(ins)
                for t in range(NT):
                    full(dve, f"mt{t}")
                    tt(HB[:, :, t * P:(t + 1) * P], ps(f"mt{t}").rearrange("p (h s) -> p h s", h=MH),
                       MO[:, :, t * P:(t + 1) * P], ALU.mult).then_inc(free(f"mt{t}"), 1)
                    moved(dve, f"mt{t}")
                dve.sem_inc(E("hb_ready"), 1)

            def silu_z(n):
                full(dve, f"gz{n}")
                dve.wait_ge(E("zsig"), n + 1)
                z2 = GZ[:, 2 * n:2 * n + 2, :]
                stt(z2, z2, VC[:, V_GG:V_GG + 1], ps(f"gz{n}").rearrange("p (c s) -> p c s", s=S), ALU.mult,
                    ALU.mult).then_inc(free(f"gz{n}"), 1)

            def solve(kind, k):
                for n in range(4):
                    full(dve, f"{kind}{k}{n}")
                    o = ps(f"{kind}{k}{n}")
                    if kind == "y":
                        ins = tt(quad(Y_[:, n, :]), quad(o), plane4(K_L0T + k), ALU.mult)
                    elif kind == "z":
                        ins = tt(X_[:, n, :], X_[:, n, :], o, ALU.subtract)
                    else:
                        ins = tt(XTi[:, n, :], XTi[:, n, :], o, ALU.subtract)
                    ins.then_inc(free(f"{kind}{k}{n}"), 1)
            conv_lru(2)
            solve("y", 1)
            conv_lru(3)
            solve("z", 1)
            solve("t", 1)
            dve.sem_inc(E("xa_ready"), 1)
            dve.sem_inc(E("lx_free"), 1)
            gelu_argument()
            solve("y", 2)
            mlstm_exponents()
            solve("z", 2)
            solve("t", 2)
            gelu()
            mlstm_scores()
            solve("y", 3)
            lru_input()
            solve("z", 3)
            solve("t", 3)
            mlstm_divide()
            lru_scan(0)
            solve("y", 4)
            lru_scan(1)
            solve("z", 4)
            mlstm_norm()
            solve("t", 4)
            solve("y", 5)
            mlstm_gate()
            silu_z(0)
            solve("t", 5)
            silu_z(1)
            branch = [f"{n}{d}" for n in range(3) for d in range(4)]

            def merge(k):
                d = k % 4
                full(dve, f"br{branch[k]}")
                moved(dve, f"ga{branch[k]}")
                m2 = MG[:, 2 * d:2 * d + 2, :].rearrange("p c s -> p (c s)")
                tt(MT[k % 2] if k >= 4 else m2, ps(f"br{branch[k]}"), SG[k % 4], ALU.mult
                   ).then_inc(free(f"br{branch[k]}"), 1)
                moved(dve, f"br{branch[k]}")
                if k >= 4:
                    step(tt(m2, m2, MT[k % 2], ALU.add))
                if k >= 8:
                    dve.sem_inc(E("merged"), 1)

            def o_squares(t):
                full(dve, f"o{t}")
                nc_v.tensor_copy(OS[:, t, :], ps(f"o{t}")).then_inc(free(f"o{t}"), 1)
                moved(dve, f"o{t}")
                step(tt(OQ[:, t, :], OS[:, t, :], OS[:, t, :], ALU.mult))
                nc_v.reduce_sum(TS[:, 8 * t:8 * t + 8], OQ[:, t, :].rearrange("p (h e) -> p h e", h=GH),
                                AX.X).then_inc(E("oss"), 1)

            def o_scale(t):
                dve.wait_ge(E("osq"), t + 1)
                step(nc_v.reciprocal(TS[:, 8 * t:8 * t + 8], TS[:, 8 * t:8 * t + 8]))
                step(tt(OQ[:, t, :].rearrange("p (h e) -> p h e", h=GH),
                        OS[:, t, :].rearrange("p (h e) -> p h e", h=GH),
                        TS[:, 8 * t:8 * t + 8].unsqueeze(2).to_broadcast([P, GH, GK]), ALU.mult))
                dve.sem_inc(E("o_norm"), 1)

            def o_gate(t):
                for n in range(2):
                    moved(dve, f"gz{n}")
                full(dve, f"ot{t}")
                tt(HC[:, :, t * P:(t + 1) * P], ps(f"ot{t}").rearrange("p (j s) -> p j s", j=GP),
                   GZ[:, :, t * P:(t + 1) * P], ALU.mult).then_inc(free(f"ot{t}"), 1)
                moved(dve, f"ot{t}")
            nc_v.memset(ST, 0.0).then_inc(E("state"), 1)
            for t in range(NT):
                moved(dve, f"u{t}")
            merge(0)
            for c in range(NC):
                t, a = c // 2, 64 * (c % 2)
                h = slice(a, a + 64)
                full(dve, f"ws{c}")
                tt(DE[h, t, :], U_[h, t, :], ps(f"ws{c}")[h], ALU.subtract).then_inc(free(f"ws{c}"), 1)
                if c < NC - 1:
                    full(dve, f"sn{c}")
                    tt(quad(STT), quad(ps(f"sn{c}")), plane4(K_BLK), ALU.mult).then_inc(free(f"sn{c}"), 1)
                    moved(dve, f"sn{c}")
                    if c == 0:
                        dve.wait_ge(E("state"), 1)
                    for j in range(GP):
                        ins = stt(ST[:, j * P:(j + 1) * P], ST[:, j * P:(j + 1) * P],
                                  EG[:, j, c * CH + CH - 1:c * CH + CH], STT[:, j * P:(j + 1) * P],
                                  ALU.mult, ALU.add)
                    ins.then_inc(E("state"), 1)
                    dve.wait_ge(E("state"), c + 2)
                merge(c + 1)
                if c == 1:
                    o_squares(0)
                if c == 2:
                    o_scale(0)
            o_squares(1)
            merge(5)
            o_gate(0)
            o_scale(1)
            merge(6)
            o_gate(1)
            dve.sem_inc(E("hc_ready"), 1)
            for k in range(7, 12):
                merge(k)
            ts(AID, ident, ALPHA, None, ALU.mult)
            nc_v.memset(YS, 0.0)
            nc_v.memset(GTS, 0.0).then_inc(E("ys_zero"), 1)
            step(nc_v.memset(POS, -1.0))
            step(nc_v.memset(GAT, 0.0))
            step(nc_v.memset(LOG[:, :, NE:], 3e38))

            BN = RT2[:, 0:24].rearrange("p (t k) -> p t k", t=NT)

            def stats(t, h, v):
                step(nc_v.bn_stats(BN[:, t, 6 * h:6 * h + 6], v))

            def normalise(n, t, y):
                v = X1[:, t, :]
                step(nc_v.bn_aggr(RT2[:, 24 + 2 * t:26 + 2 * t], BN[:, t, :]))
                nc_v.tensor_copy(TS[:, 8 + t:9 + t], RT2[:, 25 + 2 * t:26 + 2 * t]).then_inc(E(f"ln{n}_var"), 1)
                dve.wait_ge(E(f"ln{n}_in"), 32)
                step(stt(v, y, RT2[:, 24 + 2 * t:25 + 2 * t], LNG, ALU.subtract, ALU.mult))
                dve.wait_ge(E(f"ln{n}_sd"), t + 1)
                step(nc_v.reciprocal(TS[:, 8 + t:9 + t], TS[:, 8 + t:9 + t]))
                step(stt(v, v, TS[:, 8 + t:9 + t], LNB, ALU.mult, ALU.add))

            for t in range(NT):
                for h in range(2):
                    full(dve, f"wo{t}{h}")
                    v = X1[:, t, h * 512:(h + 1) * 512]
                    stt(v, XTOK[:, t, h * 512:(h + 1) * 512], ALPHA, ps(f"wo{t}{h}"), ALU.mult, ALU.add
                        ).then_inc(free(f"wo{t}{h}"), 1)
                    moved(dve, f"wo{t}{h}")
                    stats(t, h, v)
                normalise(1, t, X1[:, t, :])
                dve.sem_inc(E("x1_ready"), 1)
            dve.wait_ge(E("rout_in"), 32)
            for t in range(NT):
                full(dve, f"lgt{t}")
                tt(LOG[:, t, 0:NE], ps(f"lgt{t}")[:, 0:NE], RBIAS, ALU.add).then_inc(free(f"lgt{t}"), 1)
                moved(dve, f"lgt{t}")
                step(nc_v.max(TOP[:, t, :], LOG[:, t, 0:NE]))
                ts(EXL[:, t, :], LOG[:, t, 0:NE], TOP[:, t, 0:1], None, ALU.subtract).then_inc(E("exl_arg"), 1)
                dve.wait_ge(E("exl_arg"), t + 1)
                step(nc_v.memset(TOP[:, t, 4:8], 3e38))
                step(nc_v.match_replace(out=LOGR[:, t, :], in_to_replace=TOP[:, t, :], in_values=LOG[:, t, :],
                                        imm_value=-3e38))
                step(ts(SEL[:, t, :], LOGR[:, t, 0:NE], -2.9e38, None, ALU.is_lt))
                dve.sem_inc(E("sel_ready"), 1)
            dve.wait_ge(E("exl"), 1)
            step(tt(EXL, EXL, SEL, ALU.mult))
            step(nc_v.reduce_sum(RT2[:, 30:32], EXL, AX.X))
            step(nc_v.reciprocal(RT2[:, 30:32], RT2[:, 30:32]))
            full(dve, "cnt")
            step(stt(POS[:, :, 0:NE], ps("cnt")[:, 0:64].rearrange("p (t e) -> p t e", t=NT), 1.0, SEL, ALU.add,
                     ALU.mult))
            step(ts(POS[:, :, 0:NE], POS[:, :, 0:NE], 1.0, None, ALU.subtract))

            def onehot(i):
                for t in range(NT):
                    ins = ts(ONE[:, t, :], CM[:, K_IOTA, 0:CAP], POS[:, t, bass.ds(i, 1)], None, ALU.is_equal)
                ins.then_inc(E("onehot"), 1)

            def gated(i):
                for t in range(NT):
                    ins = ts(GAD[:, t, :], CM[:, K_IOTA], POS[:, t, bass.ds(i, 1)],
                             GAT[:, t, bass.ds(i, 1)], ALU.is_equal, ALU.mult)
                ins.then_inc(E("gated"), 1)

            def pick(e):
                nc_v.tensor_copy(PICK[0:NE, :], CM[0:NE, K_ID, bass.ds(e, 1)].to_broadcast([NE, CAP])
                                 ).then_inc(E("pick"), 1)
            onehot(0)
            step(tt(GAT[:, :, 0:NE], EXL, RT2[:, 30:32].unsqueeze(2).to_broadcast([P, NT, NE]), ALU.mult))
            dve.sem_inc(E("gates_ready"), 1)
            step(nc_v.tensor_reduce(RT2[:, 34:35], ps("cnt")[:, 64:96], AX.X, ALU.max))
            dve.sem_inc(free("cnt"), 1)
            step(ts(RT2[:, 35:36], RT2[:, 34:35], float(CAP), 1.0, ALU.is_gt, ALU.add))
            for r in range(2, ROUNDS):
                step(stt(RT2[:, 35:36], RT2[:, 34:35], float(r * CAP), RT2[:, 35:36], ALU.is_gt, ALU.add))
            nc_v.tensor_copy(NR[:, :], RT2[:, 35:36]).then_inc(E("rounds_ready"), 1)
            dve.wait_ge(E("rounds_ready"), 1)
            for r in range(1, ROUNDS):
                nc_v.tensor_copy(GAT[:, :, r * NE:(r + 1) * NE], GAT[:, :, 0:NE])
                ins = ts(POS[:, :, r * NE:(r + 1) * NE], POS[:, :, 0:NE], float(r * CAP), None, ALU.subtract)
            step(ins)
            rounds = dve.value_load(NR[0:1, 0:1], min_val=1, max_val=ROUNDS)
            with dve.Fori(0, rounds) as r, dve.Fori(0, NE) as e:
                i = r * NE + e
                pick(e)
                gated(i)
                dve.wait_ge(E("xg_full"), i + 1)
                onehot(i + 1)
                dve.wait_ge(E("chunk_used"), EC * i + KD)
                ts(GLU, PS[:, 0, :], LIMIT, None, ALU.min).then_inc(E("glu_ready"), 1)
                ts(LIN, PS[:, 1, :], -LIMIT, LIMIT, ALU.max, ALU.min).then_inc(E("lin_clipped"), 1)
                dve.wait_ge(E("glu_ready"), i + 1)
                dve.wait_ge(E("lin_clipped"), i + 1)
                stt(LIN, LIN, 1.0, GLU, ALU.add, ALU.mult).then_inc(E("lin_glu"), 1)
                dve.wait_ge(E("lin_glu"), i + 1)
                dve.wait_ge(E("sig_ready"), i + 1)
                tt(HID, LIN, SIG, ALU.mult).then_inc(E("hid_ready"), 1)
                dve.wait_ge(E("ht_full"), i + 1)
                nc_v.tensor_copy(HT, PS[:, 3, :].rearrange("p (q n) -> p q n", q=4)).then_inc(E("ht_ready"), 1)
            for t in range(NT):
                dve.wait_ge(E("acc_done"), t + 1)
                for h in range(2):
                    stats(t, h, PS[:, 4 + 2 * t + h, :])
                normalise(2, t, PS[:, 4 + 2 * t:6 + 2 * t, :].rearrange("p a b -> p (a b)"))
                dve.sem_inc(E("out_ready"), 1)


NAMES = ["x", "w_in", "lru_conv_w", "lru_conv_b", "lru_wa", "lru_ba", "lru_wx", "lru_bx", "lru_lambda",
         "ml_i_bias", "ml_f_bias", "ml_norm_g", "gd_conv_w", "gd_a_log", "gd_dt_bias", "gd_norm_g",
         "w_br_lru", "w_br_ml", "w_br_gd", "w_out", "ln1_g", "ln1_b", "router_w", "router_b",
         "exp_w1", "exp_b1", "exp_w2", "exp_b2", "ln2_g", "ln2_b"]


def kernel(**inputs):
    import concourse.bacc as bacc
    from concourse.bass_utils import run_bass_kernel_spmd

    nc = bacc.Bacc("TRN2", target_bir_lowering=False, num_devices=1)
    arrays, args = {}, []
    for name in NAMES + ["planes"]:
        a = constant_planes() if name == "planes" else np.ascontiguousarray(inputs[name])
        arrays[name] = a
        args.append(nc.dram_tensor(name, a.shape, mybir.dt.from_np(a.dtype), kind="ExternalInput").ap())
    out = nc.dram_tensor("out", (1, S, D), F32, kind="ExternalOutput").ap()
    layer_kernel(nc, *args, out)
    result = run_bass_kernel_spmd(nc, [arrays], core_ids=[0])
    return result.results[0]["out"]
```
